# Optimizing a Trainium2 kernel written in Bass

```python
import math
import jax, jax.numpy as jnp
from jax import lax
import numpy as np

D_MODEL = 1024
BATCH = 1
SEQ = 512
DEPTH = 1

CHUNK = 64
ATTN_HEADS = 8
ATTN_KV_HEADS = 2
ATTN_GROUP = ATTN_HEADS // ATTN_KV_HEADS
HEAD_DIM = D_MODEL // 16
WINDOW = 128
WINDOW_CHUNKS = WINDOW // CHUNK
ROPE_THETA = 500000.0
ROT_DIM = HEAD_DIM // 4
ATTN_SCALE = 1.0 / math.sqrt(HEAD_DIM)
HGRN_HEADS = 4
HGRN_DK = 128
HGRN_DV = (D_MODEL // 2) // HGRN_HEADS
HGRN_CHUNK = CHUNK
ATTN_Q_W = ATTN_HEADS * HEAD_DIM
ATTN_KV_W = ATTN_KV_HEADS * HEAD_DIM
HGRN_K_W = HGRN_HEADS * HGRN_DK
HGRN_V_W = HGRN_HEADS * HGRN_DV
SPLITS = (ATTN_Q_W, ATTN_KV_W, ATTN_KV_W, HGRN_K_W, HGRN_K_W, HGRN_V_W, HGRN_V_W, D_MODEL, D_MODEL)
IN_WIDTH = sum(SPLITS)
PEER_HEADS = 8
PEER_NKEYS = 128
PEER_EXPERTS = PEER_NKEYS * PEER_NKEYS
PEER_QDIM = 256
PEER_HALF = PEER_QDIM // 2
PEER_TOPK = 16
PEER_BLOCK = 128
ALPHA = (2 * DEPTH) ** 0.25
BETA = (8 * DEPTH) ** -0.25
LN_EPS = 1e-5
RMS_EPS = 1e-6
NEG_INF = -1e30

kernel_name = "hybrid_swa_hgrn2_peer_deepnorm"

def layer_norm(x, g, b):
    xf = x.astype(jnp.float32)
    mu = jnp.mean(xf, axis=-1, keepdims=True)
    var = jnp.mean(jnp.square(xf - mu), axis=-1, keepdims=True)
    y = (xf - mu) * lax.rsqrt(var + LN_EPS)
    return (y * g.astype(jnp.float32) + b.astype(jnp.float32)).astype(x.dtype)

def partial_rotary(t, positions):
    half = ROT_DIM // 2
    inv_freq = ROPE_THETA ** (-jnp.arange(0, ROT_DIM, 2, dtype=jnp.float32) / ROT_DIM)
    ang = positions.astype(jnp.float32)[..., None] * inv_freq
    cos = jnp.cos(ang)[:, :, None, :]
    sin = jnp.sin(ang)[:, :, None, :]
    tr = t[..., :ROT_DIM].astype(jnp.float32)
    t1, t2 = tr[..., :half], tr[..., half:]
    rot = jnp.concatenate([t1 * cos - t2 * sin, t2 * cos + t1 * sin], axis=-1).astype(t.dtype)
    return jnp.concatenate([rot, t[..., ROT_DIM:]], axis=-1)

def shift_chunks(t, j):
    if j == 0:
        return t
    pad = ((0, 0), (j, 0)) + ((0, 0),) * (t.ndim - 2)
    return jnp.pad(t[:, :-j], pad)

def sliding_window_gqa_sinks(q, k, v, sinks, positions):
    B, S, _ = q.shape
    nC = S // CHUNK
    q = partial_rotary(q.reshape(B, S, ATTN_HEADS, HEAD_DIM), positions)
    k = partial_rotary(k.reshape(B, S, ATTN_KV_HEADS, HEAD_DIM), positions)
    qc = q.reshape(B, nC, CHUNK, ATTN_KV_HEADS, ATTN_GROUP, HEAD_DIM)
    kc = k.reshape(B, nC, CHUNK, ATTN_KV_HEADS, HEAD_DIM)
    vc = v.reshape(B, nC, CHUNK, ATTN_KV_HEADS, HEAD_DIM)
    kb = jnp.concatenate([shift_chunks(kc, j) for j in reversed(range(WINDOW_CHUNKS))], axis=2)
    vb = jnp.concatenate([shift_chunks(vc, j) for j in reversed(range(WINDOW_CHUNKS))], axis=2)
    s = jnp.einsum('bcqhgd,bckhd->bchgqk', qc, kb).astype(jnp.float32) * ATTN_SCALE
    slot_shift = WINDOW_CHUNKS - 1 - jnp.arange(WINDOW_CHUNKS * CHUNK) // CHUNK
    valid = jnp.arange(nC)[:, None] >= slot_shift[None, :]
    s = jnp.where(valid[None, :, None, None, None, :], s, NEG_INF)
    sink = sinks.astype(jnp.float32).reshape(ATTN_KV_HEADS, ATTN_GROUP)[None, None, :, :, None, None]
    m = jnp.maximum(jnp.max(s, axis=-1, keepdims=True), sink)
    p = jnp.exp(s - m)
    w = p / (jnp.sum(p, axis=-1, keepdims=True) + jnp.exp(sink - m))
    o = jnp.einsum('bchgqk,bckhd->bcqhgd', w.astype(vb.dtype), vb)
    return o.reshape(B, S, ATTN_Q_W)

def hgrn2(q, f_logit, i, gate, lb, norm_g):
    B, S, _ = q.shape
    L = HGRN_CHUNK
    nC = S // L
    f32 = jnp.float32
    qh = jax.nn.silu(q.astype(f32)).reshape(B, nC, L, HGRN_HEADS, HGRN_DK)
    lbr = lb.reshape(HGRN_HEADS, HGRN_DK)
    fg = lbr + (1.0 - lbr) * jax.nn.sigmoid(f_logit.astype(f32).reshape(B, nC, L, HGRN_HEADS, HGRN_DK))
    kh = 1.0 - fg
    bcum = jnp.cumsum(jnp.log(fg), axis=2)
    vh = i.astype(f32).reshape(B, nC, L, HGRN_HEADS, HGRN_DV)
    q_ = qh * jnp.exp(bcum)
    k_ = kh * jnp.exp(-bcum)
    A = jnp.einsum('bclhk,bcshk->bchls', q_, k_)
    A = jnp.where(jnp.tril(jnp.ones((L, L), dtype=bool)), A, 0.0)
    o_intra = jnp.einsum('bchls,bcshv->bclhv', A, vh)
    b_last = bcum[:, :, -1]
    k_end = kh * jnp.exp(b_last[:, :, None] - bcum)
    kv = jnp.einsum('bcshk,bcshv->bchkv', k_end, vh)
    decay = jnp.exp(b_last)

    def step(state, inp):
        d, kvc = inp
        return d[..., None] * state + kvc, state

    init = jnp.zeros((B, HGRN_HEADS, HGRN_DK, HGRN_DV), f32)
    _, s_prev = lax.scan(step, init, (jnp.moveaxis(decay, 1, 0), jnp.moveaxis(kv, 1, 0)))
    s_prev = jnp.moveaxis(s_prev, 0, 1)
    o = o_intra + jnp.einsum('bclhk,bchkv->bclhv', q_, s_prev)
    o = o.reshape(B, S, HGRN_HEADS, HGRN_DV)
    o = o * lax.rsqrt(jnp.mean(jnp.square(o), axis=-1, keepdims=True) + RMS_EPS) * norm_g.astype(f32)
    o = o * jax.nn.silu(gate.astype(f32).reshape(B, S, HGRN_HEADS, HGRN_DV))
    return o.reshape(B, S, HGRN_V_W).astype(q.dtype)

def peer_ffn(x, wq, keys, u, v):
    B, S, D = x.shape
    T = B * S
    xb = x.reshape(T // PEER_BLOCK, PEER_BLOCK, D)
    f32 = jnp.float32

    def block(xt):
        q = (xt @ wq).reshape(PEER_BLOCK, PEER_HEADS, 2, PEER_HALF).astype(f32)
        s1 = jnp.einsum('thd,kd->thk', q[:, :, 0], keys[0].astype(f32))
        s2 = jnp.einsum('thd,kd->thk', q[:, :, 1], keys[1].astype(f32))
        v1, i1 = lax.top_k(s1, PEER_TOPK)
        v2, i2 = lax.top_k(s2, PEER_TOPK)
        cand = (v1[..., :, None] + v2[..., None, :]).reshape(PEER_BLOCK, PEER_HEADS, PEER_TOPK * PEER_TOPK)
        sc, ci = lax.top_k(cand, PEER_TOPK)
        e = (jnp.take_along_axis(i1, ci // PEER_TOPK, axis=-1) * PEER_NKEYS
             + jnp.take_along_axis(i2, ci % PEER_TOPK, axis=-1))
        g = jax.nn.softmax(sc, axis=-1)
        hid = jnp.einsum('thkd,td->thk', u[e], xt)
        act = jax.nn.gelu(hid.astype(f32), approximate=False)
        out = jnp.einsum('thk,thkd->td', (g * act).astype(v.dtype), v[e])
        return out.astype(xt.dtype)

    return lax.map(block, xb).reshape(B, S, D)

def setup_inputs(seed: int = 0) -> dict:
    key = jax.random.key(seed)
    ks = jax.random.split(key, 20)
    nrm = jax.random.normal
    x = nrm(ks[0], (BATCH, SEQ, D_MODEL), jnp.float32)
    positions = (jax.random.randint(ks[1], (BATCH, 1), 0, 65536, dtype=jnp.int32)
                 + jnp.arange(SEQ, dtype=jnp.int32)[None, :])
    col_scales = (1.0, 1.0, BETA, 1.0, 1.0, BETA, 1.0, 1.0, 1.0)
    col_scale = jnp.concatenate([jnp.full((w,), s, jnp.float32) for w, s in zip(SPLITS, col_scales)])
    w_in = nrm(ks[2], (DEPTH, D_MODEL, IN_WIDTH), jnp.float32) * D_MODEL ** -0.5 * col_scale
    attn_sinks = 0.5 * nrm(ks[3], (DEPTH, ATTN_HEADS), jnp.float32)
    hgrn_lb = 0.1 * nrm(ks[4], (DEPTH + 1, HGRN_K_W), jnp.float32)
    hgrn_norm_g = 1.0 + 0.02 * nrm(ks[5], (DEPTH, HGRN_DV), jnp.float32)
    w_proj_attn = nrm(ks[6], (DEPTH, ATTN_Q_W, D_MODEL), jnp.float32) * ATTN_Q_W ** -0.5 * BETA
    w_proj_hgrn = nrm(ks[7], (DEPTH, HGRN_V_W, D_MODEL), jnp.float32) * HGRN_V_W ** -0.5 * BETA
    w_out = nrm(ks[8], (DEPTH, D_MODEL, D_MODEL), jnp.float32) * D_MODEL ** -0.5 * BETA
    ln1_g = 1.0 + 0.02 * nrm(ks[9], (DEPTH, D_MODEL), jnp.float32)
    ln1_b = 0.02 * nrm(ks[10], (DEPTH, D_MODEL), jnp.float32)
    peer_wq = nrm(ks[11], (DEPTH, D_MODEL, PEER_HEADS * PEER_QDIM), jnp.float32) * D_MODEL ** -0.5
    peer_keys = nrm(ks[12], (DEPTH, 2, PEER_NKEYS, PEER_HALF), jnp.float32) * PEER_HALF ** -0.5
    peer_u = nrm(ks[13], (DEPTH, PEER_EXPERTS, D_MODEL), jnp.float32) * D_MODEL ** -0.5
    peer_v = nrm(ks[14], (DEPTH, PEER_EXPERTS, D_MODEL), jnp.float32) * BETA
    ln2_g = 1.0 + 0.02 * nrm(ks[15], (DEPTH, D_MODEL), jnp.float32)
    ln2_b = 0.02 * nrm(ks[16], (DEPTH, D_MODEL), jnp.float32)
    return {"x": x, "positions": positions, "w_in": w_in, "attn_sinks": attn_sinks,
            "hgrn_lb": hgrn_lb, "hgrn_norm_g": hgrn_norm_g, "w_proj_attn": w_proj_attn,
            "w_proj_hgrn": w_proj_hgrn, "w_out": w_out, "ln1_g": ln1_g, "ln1_b": ln1_b,
            "peer_wq": peer_wq, "peer_keys": peer_keys, "peer_u": peer_u, "peer_v": peer_v,
            "ln2_g": ln2_g, "ln2_b": ln2_b}

def reference(x, positions, w_in, attn_sinks, hgrn_lb, hgrn_norm_g, w_proj_attn, w_proj_hgrn,
              w_out, ln1_g, ln1_b, peer_wq, peer_keys, peer_u, peer_v, ln2_g, ln2_b):
    split_points = []
    acc = 0
    for w in SPLITS[:-1]:
        acc += w
        split_points.append(acc)
    lb_all = jnp.cumsum(jax.nn.softmax(hgrn_lb.astype(jnp.float32), axis=0), axis=0)
    for l in range(DEPTH):
        proj = jnp.einsum('bsd,de->bse', x, w_in[l])
        aq, ak, av, hq, hf, hi, hg, ga, gh = jnp.split(proj, split_points, axis=-1)
        attn = sliding_window_gqa_sinks(aq, ak, av, attn_sinks[l], positions)
        rec = hgrn2(hq, hf, hi, hg, lb_all[l], hgrn_norm_g[l])
        mixed = (jax.nn.sigmoid(ga) * (attn @ w_proj_attn[l])
                 + jax.nn.sigmoid(gh) * (rec @ w_proj_hgrn[l]))
        x = layer_norm(ALPHA * x + mixed @ w_out[l], ln1_g[l], ln1_b[l])
        ffn = peer_ffn(x, peer_wq[l], peer_keys[l], peer_u[l], peer_v[l])
        x = layer_norm(ALPHA * x + ffn, ln2_g[l], ln2_b[l])
    return x


_drawn_inputs = setup_inputs


def setup_inputs(seed=0):
    import zlib

    import numpy as np

    out = dict(_drawn_inputs(seed))
    spreads = {}
    factors = {'attn_sinks': 24.554, 'hgrn_lb': 6.108, 'hgrn_norm_g': 4.515, 'ln2_g': 8.19, 'ln2_b': 8.18}
    for name, (base, spread) in spreads.items():
        noise = np.random.default_rng([zlib.crc32(name.encode()), seed]).standard_normal(out[name].shape)
        drawn = base * np.exp(spread * noise) if base else spread * noise
        out[name] = __import__('jax').numpy.asarray(drawn.astype(out[name].dtype))
    for name, factor in factors.items():
        out[name] = (out[name] * factor).astype(out[name].dtype)
    return out
```

```python
import math
from contextlib import ExitStack

import concourse.bass as bass
from concourse import mybir

P = 128
F32 = mybir.dt.float32
U32 = mybir.dt.uint32
I32 = mybir.dt.int32
ALU = mybir.AluOpType
ACT = mybir.ActivationFunctionType
AX_X = mybir.AxisListType.X

S, D = 512, 1024
T = S // P
KC = D // P
CH = 64
NC = S // CH
HEADS, KVH, HD = 8, 2, 64
PAIRS = HEADS // 2
ROT = HD // 4
HALF = ROT // 2
HH, DK, DV = 4, 128, 128
TOKW = HEADS * HD + 2 * KVH * HD + 2 * HH * DV
TG = 4
TGW = TOKW // TG
K0 = HEADS * HD
V0 = K0 + KVH * HD
I0 = V0 + KVH * HD
G0 = I0 + HH * DV
PH, NK, TOPK = 8, 128, 16
NE = PH * TOPK
SCALE = 1.0 / math.sqrt(HD)
NEG = -1e30
LOWEST = -3.0e38
PER_TILE = 152
ALPHA = 2.0 ** 0.25
LN_EPS = 1e-5
RMS_EPS = 1e-6

RING = 3
ITEM_TOK, ITEM_HQ, ITEM_HF, ITEM_MIX, ITEM_OUT, ITEM_WQ, ITEMS = 0, 4, 5, 6, 14, 16, 20
MIXW = (2 * KC + 2 * HH) * P

SLOTS, GRP = 16, 4
GPR = SLOTS // GRP
ROUNDS = NE // SLOTS
GPP = GPR * ROUNDS

PI2_A = 6.28125
PI2_B = math.floor((2 * math.pi - PI2_A) * 2 ** 19) / 2 ** 19
PI2_C = 2 * math.pi - PI2_A - PI2_B
MAGIC = 1.5 * 2 ** 23


def build(nc, x, xT, w_tok, w_hqf, w_mix, w_out, w_q, keysT, pos, inv_freq, sinks, lb_logits, norm_g,
          ln1, ln2, ident_d, causal_d, chunk_d, iota_d, u_rows, v_rows, out):
    with ExitStack() as ctx:
        def sb(name, shape, dt=F32):
            return ctx.enter_context(nc.sbuf_tensor(name, shape, dt))

        def sem(name):
            return ctx.enter_context(nc.semaphore(name))

        KB = 256
        arena = sb("arena", [P, 184 * KB])

        def view(kb, *dims, parts=P, dt=F32):
            n = 1
            for d in dims:
                n *= d
            a = arena[0:parts, int(kb * KB):int(kb * KB) + n]
            if dt != F32:
                a = a.bitcast(dt)
            if len(dims) == 1:
                return a
            names = "abcd"[:len(dims)]
            return a.rearrange(f"p ({' '.join(names)}) -> p {' '.join(names)}",
                               **{k: d for k, d in zip(names[1:], dims[1:])})

        ring = view(0, RING, 4096)
        act_in = view(48, KC, S)
        tok = view(64, T, TOKW)
        qT = view(92, NC, HEADS, CH, parts=HD)
        PT = view(92, NC, PAIRS, P)
        kT = view(108, KVH, S, parts=HD)
        SC = view(112, NC, PAIRS, P)
        ST = view(112, NC, HH, DV)
        mixT = view(112, KC, S)
        attnT = view(128, PAIRS, S)
        recT = view(136, HH, S)
        HQ = view(144, HH, S)
        HF = view(152, HH, S)
        SQ = view(160, HH, S)
        KH = view(168, HH, S)
        BC = view(176, HH, S)
        kendT = view(92, T, HH, DK)
        AT = view(100, T, HH, P)
        otok = view(168, T, HH, DV)
        v_even = view(160, T, KVH * HD)
        v_odd = view(162, T, KVH * HD)
        sig = view(144, 2, 2, S)
        osq = view(160, HH, DV)
        rot = view(176, 4, T, (HEADS + KVH), HALF)
        ln_gb = view(176, 2, D)
        qTp = view(64, 2 * PH, S)
        s12 = view(112, T, 2 * PH * NK)
        rows = view(0, SLOTS, D)
        x1cur = view(64, D)
        ybuf = view(68, D)
        diag = view(72, SLOTS, P)
        scur = view(144, 2 * PH, NK)
        cand = view(152, PH, TOPK, TOPK)
        onehot = view(160, NE, TOPK)
        picked = view(168, NE, TOPK)
        cur = view(80, SLOTS, dt=U32)
        eidx = view(80.125, T, NE, dt=U32)
        top = view(82.125, PH, 2, TOPK)
        topi = view(83.125, PH, 2, TOPK, dt=U32)
        topf = view(84.125, PH, 2, TOPK)
        sco = view(85.125, PH, TOPK)
        sci = view(85.625, PH, TOPK, dt=U32)
        half_i = view(86.125, PH, TOPK, dt=U32)
        half_f = view(86.625, PH, TOPK)
        e1 = view(87.125, NE)
        e2 = view(87.625, NE)
        gexp = view(88.125, PH, TOPK)
        gsum = view(88.625, PH)
        hid_r = view(88.75, SLOTS)
        hid = view(88.875, NE)
        wv = view(89.375, NE)

        x1 = sb("x1", [P, T, D])
        ident = sb("ident", [P, P])
        alphaI = sb("alphaI", [P, P])
        causal = sb("causal", [P, P], U32)
        chunk_mask = sb("chunk_mask", [P, S])
        iota16 = sb("iota16", [P, TOPK])
        keys = sb("keys", [P, 2, NK])
        normg = sb("normg", [P, DV])
        pos_i = sb("pos_i", [P, T], I32)
        pos_f = sb("pos_f", [P, T])
        freq = sb("freq", [P, HALF])
        sinkc = sb("sinkc", [P, PAIRS])
        lbl = sb("lbl", [P, 2, HH])
        lbm = sb("lbm", [P, HH])
        lbv = sb("lbv", [P, HH])
        omlb = sb("omlb", [P, HH])
        ang = sb("ang", [P, T, HALF])
        turns = sb("turns", [P, T, HALF])
        trig = sb("trig", [P, 2, T, HALF])
        mx = sb("mx", [P, NC, PAIRS])
        snk = sb("snk", [P, NC, PAIRS])
        den = sb("den", [P, NC, PAIRS])
        decay = sb("decay", [P, HH, NC])
        rms = sb("rms", [P, T, HH])
        stats = sb("stats", [P, 2, 6])
        mv = sb("mv", [P, 2])
        rstd = sb("rstd", [P, 1])
        bank = ctx.enter_context(nc.psum_tensor("bank", [P, 8, 512], F32))

        xT_in = sem("xT_in")
        x_in = sem("x_in")
        consts_in = sem("consts_in")
        ln1_in = sem("ln1_in")
        ln2_in = sem("ln2_in")
        w_in = [sem(f"w_in{i}") for i in range(RING)]
        proj_done = sem("proj_done")
        proj_out = sem("proj_out")
        trig_arg = sem("trig_arg")
        trig_ready = sem("trig_ready")
        lb_arg = sem("lb_arg")
        lb_exp = sem("lb_exp")
        rope_done = sem("rope_done")
        qk_turned = sem("qk_turned")
        qk_out = sem("qk_out")
        score_done = sem("score_done")
        score_out = sem("score_out")
        soft_arg = sem("soft_arg")
        soft_exp = sem("soft_exp")
        soft_done = sem("soft_done")
        w_turned = sem("w_turned")
        w_outT = sem("w_outT")
        av_done = sem("av_done")
        av_out = sem("av_out")
        hgrn_act = sem("hgrn_act")
        fg_ready = sem("fg_ready")
        bcum_ready = sem("bcum_ready")
        kq_ready = sem("kq_ready")
        kend_turned = sem("kend_turned")
        kend_out = sem("kend_out")
        at_done = sem("at_done")
        at_out = sem("at_out")
        kv_done = sem("kv_done")
        state_ready = sem("state_ready")
        o_done = sem("o_done")
        ms_ready = sem("ms_ready")
        rms_root = sem("rms_root")
        rec_ready = sem("rec_ready")
        rec_turned = sem("rec_turned")
        rec_out = sem("rec_out")
        mix_done = sem("mix_done")
        gate_ready = sem("gate_ready")
        mix_out = sem("mix_out")
        y_done = sem("y_done")
        y_out = sem("y_out")
        var_ready = sem("var_ready")
        std_ready = sem("std_ready")
        x1_ready = sem("x1_ready")
        x1_turned = sem("x1_turned")
        x1_out = sem("x1_out")
        pq_done = sem("pq_done")
        pq_out = sem("pq_out")
        ks_done = sem("ks_done")
        ks_out = sem("ks_out")
        step = sem("step")
        route_gate = sem("route_gate")
        idx_ready = sem("idx_ready")
        gexp_arg = sem("gexp_arg")
        gexp_done = sem("gexp_done")
        cur_ready = sem("cur_ready")
        pool_gate = sem("pool_gate")
        landed = [sem(f"landed{i}") for i in range(SLOTS)]
        u_used = sem("u_used")
        v_used = sem("v_used")
        hid_ready = sem("hid_ready")
        gelu_done = sem("gelu_done")
        wv_ready = sem("wv_ready")
        act_gate = sem("act_gate")
        diag_ready = sem("diag_ready")
        acc_out = sem("acc_out")
        y2_ready = sem("y2_ready")
        y_free = sem("y_free")
        out_done = sem("out_done")
        alpha_ready = sem("alpha_ready")

        CONSTS = 13
        GATES = 3

        def item_in(eng, n):
            eng.wait_ge(w_in[n % RING], 16 * (n // RING + 1))

        class Chain:

            def __init__(self, eng):
                self.eng, self.n, self.dyn = eng, 0, []

            def value(self):
                v = self.n
                for i, n0, per in self.dyn:
                    v = i * per + v
                return v

            def __call__(self, ins):
                ins.then_inc(step, 1)
                self.n += 1
                return ins

            def wait(self):
                self.eng.wait_ge(step, self.value())

            def gate(self):
                self.wait()
                self.eng.sem_inc(route_gate, 1)

            def enter(self, i, per):
                self.dyn.append((i, self.n, per))

            def leave(self, times):
                _, n0, per = self.dyn.pop()
                assert self.n - n0 == per, (self.n - n0, per)
                self.n = n0 + per * times

        block = ctx.enter_context(nc.Block())

        @block.sync
        def _(sp):
            sp.dma_start(act_in, xT.rearrange("(c p) t -> p c t", p=P)).then_inc(xT_in, 16)

            def load(n):
                if n >= RING:
                    old = n - RING
                    if old < ITEM_MIX:
                        sp.wait_ge(proj_done, 4 * (old + 1))
                    elif old < ITEM_OUT:
                        sp.wait_ge(mix_done, old - ITEM_MIX + 1)
                    elif old < ITEM_WQ:
                        sp.wait_ge(y_done, 2 * T - 1 + (old - ITEM_OUT))
                    else:
                        sp.wait_ge(pq_done, 4 * (old - ITEM_WQ + 1))
                dst = ring[:, n % RING, :]
                if n < ITEM_HQ:
                    src, dst = w_tok[n], dst[:, 0:KC * TGW]
                elif n < ITEM_MIX:
                    src = w_hqf[n - ITEM_HQ]
                elif n < ITEM_OUT:
                    src, dst = w_mix[n - ITEM_MIX], dst[:, 0:MIXW]
                elif n < ITEM_WQ:
                    src = w_out[n - ITEM_OUT]
                else:
                    src = w_q[n - ITEM_WQ]
                sp.dma_start(dst, src).then_inc(w_in[n % RING], 16)

            load(0)
            for dst, src in ((ident[:, :], ident_d), (causal[:, :], causal_d), (chunk_mask[:, :], chunk_d),
                             (iota16[:, :], iota_d), (keys[:, :, :], keysT), (pos_i[:, :], pos),
                             (lbl[:, :, :], lb_logits), (freq[:, :], inv_freq.partition_broadcast(P)),
                             (normg[:, :], norm_g.partition_broadcast(P))):
                sp.dma_start(dst, src).then_inc(consts_in, 16)
            for hh in range(2):
                sp.dma_start(sinkc[CH * hh:CH * hh + CH, :], sinks[hh, :].partition_broadcast(CH)).then_inc(consts_in, 16)
            load(1)
            load(2)
            sp.dma_start(x1[:, :, :], x.rearrange("(t p) d -> p t d", p=P)).then_inc(x_in, 16)
            for n in range(3, ITEM_MIX + 1):
                load(n)
            sp.wait_ge(kq_ready, 1)
            for k in range(2):
                sp.dma_start(ln_gb[:, k, :], ln1[k, :].partition_broadcast(P)).then_inc(ln1_in, 16)
            for n in range(ITEM_MIX + 1, ITEMS):
                load(n)
            sp.wait_ge(x1_ready, T)
            for k in range(2):
                sp.dma_start(ln_gb[:, k, :], ln2[k, :].partition_broadcast(P)).then_inc(ln2_in, 16)
            sp.sem_inc(y_free, 1)
            with sp.Fori(0, T) as t:
                sp.wait_ge(y2_ready, t + 1)
                sp.dma_start(out[bass.ds(t * P, P), :], ybuf).then_inc(out_done, 16)
                sp.wait_ge(out_done, 16 * (t + 1))
                sp.sem_inc(y_free, 1)
            sp.wait_ge(out_done, 16 * T)

        @block.tensor
        def _(pe):
            mm = nc.tensor.matmul
            pe.wait_ge(xT_in, 16)

            for g in range(TG):
                item_in(pe, g)
                w = ring[:, g % RING, 0:KC * TGW].rearrange("p (c n) -> p c n", c=KC)
                for t in range(T):
                    b = g * T + t
                    if b >= 4:
                        pe.wait_ge(proj_out, b - 3)
                    for c in range(KC):
                        last = mm(bank[:, b % 4, 0:TGW], act_in[:, c, t * P:(t + 1) * P], w[:, c, :],
                                  start=c == 0, stop=c == KC - 1)
                    last.then_inc(proj_done, 1)

            pe.wait_ge(consts_in, 16 * (CONSTS - 2))
            pe.wait_ge(rope_done, 1)
            for t in range(T):
                for part in range(3):
                    u = 3 * t + part
                    if u >= 3:
                        pe.wait_ge(qk_out, u - 2)
                    for k in range(4 if part < 2 else 2):
                        h = 4 * part + k
                        last = nc.tensor.transpose(bank[0:HD, 4 + u % 3, k * P:(k + 1) * P],
                                                   tok[:, t, h * HD:(h + 1) * HD], ident[:, :])
                    last.then_inc(qk_turned, 1)

            pe.wait_ge(qk_out, 3 * T)
            for c in range(NC):
                if c >= 4:
                    pe.wait_ge(score_out, c - 3)
                for j in range(PAIRS):
                    g = j // (PAIRS // KVH)
                    q = qT[:, c, 2 * j:2 * j + 2, :]
                    o = bank[:, 4 + c % 4, j * P:(j + 1) * P]
                    if c % 2:
                        last = mm(o, q, kT[:, g, (c - 1) * CH:(c + 1) * CH], start=True, stop=True)
                    else:
                        last = mm(o[:, 0:CH], q, kT[:, g, c * CH:(c + 1) * CH], start=True, stop=True)
                        if c:
                            last = mm(o[:, CH:P], q, kT[:, g, (c - 1) * CH:c * CH], start=True, stop=True)
                last.then_inc(score_done, 1)

            for b in range(4 * TG, 4 * TG + 8):
                n = ITEM_HQ + (b - 4 * TG) // 4
                item_in(pe, n)
                w = ring[:, n % RING, :].rearrange("p (c n) -> p c n", c=KC)
                pe.wait_ge(proj_out, b - 3)
                for c in range(KC):
                    last = mm(bank[:, b % 4, :], w[:, c, b % 4 * P:(b % 4 + 1) * P], act_in[:, c, :],
                              start=c == 0, stop=c == KC - 1)
                last.then_inc(proj_done, 1)

            def turn_weights(c):
                if c >= 2:
                    pe.wait_ge(w_outT, c - 1)
                for j in range(PAIRS):
                    last = nc.tensor.transpose(bank[:, 4 + c % 2, j * P:(j + 1) * P], SC[:, c, j, :], ident[:, :])
                last.then_inc(w_turned, 1)

            def times_v(c):
                pe.wait_ge(w_outT, c + 1)
                if c >= 2:
                    pe.wait_ge(av_out, c - 1)
                for j in range(PAIRS):
                    g = j // (PAIRS // KVH)
                    vc = slice(V0 + g * HD, V0 + (g + 1) * HD)
                    for hh in range(2):
                        o = bank[hh * HD:(hh + 1) * HD, 6 + c % 2, j * CH:(j + 1) * CH]
                        p = PT[:, c, j, hh * CH:(hh + 1) * CH]
                        if c % 2:
                            last = mm(o, tok[:, c // 2, vc], p, start=True, stop=True)
                        else:
                            vz = slice(g * HD, (g + 1) * HD)
                            last = mm(o, v_even[:, c // 2, vz], p, start=True, stop=c == 0)
                            if c:
                                last = mm(o, v_odd[:, c // 2 - 1, vz], p, start=False, stop=True)
                last.then_inc(av_done, 1)

            pe.wait_ge(soft_done, 1)
            turn_weights(0)
            for c in range(NC):
                if c + 1 < NC:
                    turn_weights(c + 1)
                times_v(c)

            pe.wait_ge(kq_ready, 1)
            pe.wait_ge(av_out, NC)
            for t in range(T):
                if t >= 2:
                    pe.wait_ge(kend_out, t - 1)
                for h in range(HH):
                    last = nc.tensor.transpose(bank[:, 4 + t % 2, h * P:(h + 1) * P],
                                               HF[:, h, t * P:(t + 1) * P], ident[:, :])
                last.then_inc(kend_turned, 1)
                if t >= 2:
                    pe.wait_ge(at_out, t - 1)
                tokens = slice(t * P, (t + 1) * P)
                for h in range(HH):
                    last = mm(bank[:, 6 + t % 2, h * P:(h + 1) * P], KH[:, h, tokens], HQ[:, h, tokens],
                              start=True, stop=True)
                last.then_inc(at_done, 1)

            def chunk_kv(c):
                t, cc = c // 2, c % 2
                pe.wait_ge(kend_out, t + 1)
                if c >= 2:
                    pe.wait_ge(state_ready, c)
                for h in range(HH):
                    last = mm(bank[:, c % 2, h * DV:(h + 1) * DV], kendT[cc * CH:(cc + 1) * CH, t, h, :],
                              tok[cc * CH:(cc + 1) * CH, t, I0 + h * DV:I0 + (h + 1) * DV], start=True, stop=True)
                last.then_inc(kv_done, 1)

            def tile_out(t):
                pe.wait_ge(at_out, t + 1)
                if t >= 2:
                    pe.wait_ge(rec_ready, t - 1)
                pe.wait_ge(state_ready, 2 * t + 2)
                for h in range(HH):
                    hv = slice(h * DV, (h + 1) * DV)
                    mm(bank[:, 2 + t % 2, hv], AT[:, t, h, :], tok[:, t, I0 + h * DV:I0 + (h + 1) * DV],
                       start=True, stop=False, skip_group_check=True)
                    for cc in range(2):
                        c = 2 * t + cc
                        last = mm(bank[cc * CH:(cc + 1) * CH, 2 + t % 2, hv], HQ[:, h, c * CH:(c + 1) * CH],
                                  ST[:, c, h, :], start=False, stop=True, skip_group_check=True)
                last.then_inc(o_done, 1)

            def turn_rec(t):
                pe.wait_ge(rec_ready, t + 1)
                if t >= 2:
                    pe.wait_ge(rec_out, t - 1)
                for h in range(HH):
                    last = nc.tensor.transpose(bank[:, 4 + t % 2, h * P:(h + 1) * P], otok[:, t, h, :], ident[:, :])
                last.then_inc(rec_turned, 1)

            chunk_kv(0)
            for t in range(T):
                chunk_kv(2 * t + 1) if 2 * t + 1 < NC - 1 else None
                tile_out(t)
                if 2 * t + 2 < NC - 1:
                    chunk_kv(2 * t + 2)
                if t >= 1:
                    turn_rec(t - 1)
            turn_rec(T - 1)

            pe.wait_ge(rec_out, T)
            for m in range(KC):
                item_in(pe, ITEM_MIX + m)
                w = ring[:, (ITEM_MIX + m) % RING, 0:MIXW].rearrange("p (c n) -> p c n", n=P)
                if m >= 2:
                    pe.wait_ge(mix_out, m - 1)
                b = 4 * (m % 2)
                for c in range(KC):
                    mm(bank[:, b, :], w[:, c, :], act_in[:, c, :], start=c == 0, stop=c == KC - 1)
                for c in range(KC):
                    mm(bank[:, b + 1, :], w[:, KC + c, :], act_in[:, c, :], start=c == 0, stop=c == KC - 1)
                for j in range(PAIRS):
                    mm(bank[:, b + 2, :], w[:, 2 * KC + j, :], attnT[:, j, :], start=j == 0, stop=j == PAIRS - 1)
                for h in range(HH):
                    last = mm(bank[:, b + 3, :], w[:, 2 * KC + PAIRS + h, :], recT[:, h, :],
                              start=h == 0, stop=h == HH - 1)
                last.then_inc(mix_done, 1)

            pe.wait_ge(mix_out, KC)
            item_in(pe, ITEM_OUT)
            item_in(pe, ITEM_OUT + 1)
            for t in range(T):
                for n in range(2):
                    u = 2 * t + n
                    w = ring[:, (ITEM_OUT + n) % RING, :].rearrange("p (c n) -> p c n", c=KC)
                    if u >= 4:
                        pe.wait_ge(y_out, u - 3)
                    for c in range(KC):
                        last = mm(bank[:, u % 4, :], mixT[:, c, t * P:(t + 1) * P], w[:, c, :],
                                  start=c == 0, stop=c == KC - 1)
                    last.then_inc(y_done, 1)

            for t in range(T):
                pe.wait_ge(x1_ready, t + 1)
                for n in range(2):
                    u = 2 * t + n
                    if u >= 4:
                        pe.wait_ge(x1_out, u - 3)
                    for k in range(4):
                        c = 4 * n + k
                        last = nc.tensor.transpose(bank[:, 4 + u % 4, k * P:(k + 1) * P],
                                                   x1[:, t, c * P:(c + 1) * P], ident[:, :])
                    last.then_inc(x1_turned, 1)

            pe.wait_ge(x1_out, 2 * T)
            pe.wait_ge(y_out, 2 * T)
            for b in range(2 * PH):
                n = ITEM_WQ + b // 4
                item_in(pe, n)
                w = ring[:, n % RING, :].rearrange("p (c n) -> p c n", c=KC)
                if b >= 4:
                    pe.wait_ge(pq_out, b - 3)
                for c in range(KC):
                    last = mm(bank[:, b % 4, :], w[:, c, b % 4 * P:(b % 4 + 1) * P], act_in[:, c, :],
                              start=c == 0, stop=c == KC - 1)
                last.then_inc(pq_done, 1)

            pe.wait_ge(pq_out, 2 * PH)
            for u in range(4 * T):
                t, quad = u // 4, u % 4
                if u >= 4:
                    pe.wait_ge(ks_out, u - 3)
                for k in range(4):
                    b = 4 * quad + k
                    last = mm(bank[:, 4 + u % 4, k * NK:(k + 1) * NK], qTp[:, b, t * P:(t + 1) * P],
                              keys[:, b % 2, :], start=True, stop=True)
                last.then_inc(ks_done, 1)

            pe.wait_ge(alpha_ready, 1)
            pe.wait_ge(ks_out, 4 * T)

            def v_round(t, i):
                for s in range(SLOTS):
                    if s % GRP == 0:
                        pe.wait_ge(diag_ready, GPP * t + GPR * i + s // GRP + 1)
                    pe.wait_ge(landed[s], 16 * (2 * ROUNDS * t + ROUNDS + i + 1))
                    mm(bank[:, 0, :], diag[:, s, :], rows[:, s, 0:512], start=False, stop=False, skip_group_check=True)
                    last = mm(bank[:, 1, :], diag[:, s, :], rows[:, s, 512:D], start=False, stop=False,
                              skip_group_check=True)
                    if s % GRP == GRP - 1:
                        last.then_inc(v_used, 1)

            with pe.Fori(0, T) as t:
                pe.wait_ge(acc_out, t + 1)
                for n in range(2):
                    mm(bank[:, n, :], alphaI[:, :], x1.rearrange("p t d -> p (t d)")[:, bass.ds(t * D + n * 512, 512)],
                       start=True, stop=False, skip_group_check=True)
                with pe.Fori(0, ROUNDS) as i:
                    v_round(t, i)

        @block.scalar
        def _(act):
            fn = nc.scalar.activation

            def copy_x1(u):
                act.wait_ge(x1_turned, u + 1)
                fn(act_in[:, u % 2 * 4:u % 2 * 4 + 4, u // 2 * P:(u // 2 + 1) * P],
                   bank[:, 4 + u % 4, :].rearrange("p (c k) -> p c k", c=4), ACT.Copy).then_inc(x1_out, 1)

            act.wait_ge(lb_arg, 1)
            fn(lbl[:, :, :], lbl[:, :, :], ACT.Exp).then_inc(lb_exp, 1)
            act.wait_ge(trig_arg, 1)
            fn(trig[:, :, :, :], trig[:, :, :, :], ACT.Sin).then_inc(trig_ready, 1)

            def copy_tok(b):
                g, t = b // T, b % T
                act.wait_ge(proj_done, b + 1)
                fn(tok[:, t, g * TGW:(g + 1) * TGW], bank[:, b % 4, 0:TGW], ACT.Copy).then_inc(proj_out, 1)

            for b in range(4 * TG):
                copy_tok(b)
            act.wait_ge(soft_arg, 1)
            fn(SC, SC, ACT.Exp).then_inc(soft_exp, 1)
            fn(snk[:, :, :], snk[:, :, :], ACT.Exp).then_inc(soft_exp, 1)
            for k in range(8):
                act.wait_ge(proj_done, 4 * TG + k + 1)
                dst = HQ if k < 4 else HF
                fn(dst[:, k % 4, :], bank[:, k % 4, :], ACT.Copy).then_inc(proj_out, 1)
            act.wait_ge(proj_out, 4 * TG + 8)
            fn(HQ, HQ, ACT.Silu).then_inc(hgrn_act, 1)
            gate = tok[:, :, G0:G0 + HH * DV]
            fn(gate, gate, ACT.Silu).then_inc(hgrn_act, 1)
            fn(HF, HF, ACT.Sigmoid).then_inc(hgrn_act, 1)
            for c in range(NC):
                act.wait_ge(w_turned, c + 1)
                fn(PT[:, c, :, :], bank[:, 4 + c % 2, :].rearrange("p (j k) -> p j k", j=PAIRS),
                   ACT.Copy).then_inc(w_outT, 1)
            for h in range(HH):
                act.wait_ge(fg_ready, h + 1)
                fn(HF[:, h, :], HF[:, h, :], ACT.Ln).then_inc(hgrn_act, 1)
            act.wait_ge(bcum_ready, 1)
            fn(SQ, BC, ACT.Exp).then_inc(hgrn_act, 1)
            fn(HF, HF, ACT.Exp).then_inc(hgrn_act, 1)
            act.wait_ge(hgrn_act, GATES + HH + 1)
            fn(BC, BC, ACT.Exp, scale=-1.0).then_inc(hgrn_act, 1)
            for t in range(T):
                act.wait_ge(kend_turned, t + 1)
                fn(kendT[:, t, :, :], bank[:, 4 + t % 2, :].rearrange("p (h k) -> p h k", h=HH),
                   ACT.Copy).then_inc(kend_out, 1)

            def root_rms(t):
                act.wait_ge(ms_ready, t + 1)
                fn(rms[:, t, :], rms[:, t, :], ACT.Sqrt).then_inc(rms_root, 1)

            def copy_rec(t):
                act.wait_ge(rec_turned, t + 1)
                fn(recT[:, :, t * P:(t + 1) * P], bank[:, 4 + t % 2, :].rearrange("p (h k) -> p h k", h=HH),
                   ACT.Copy).then_inc(rec_out, 1)

            root_rms(0)
            for t in range(1, T):
                root_rms(t)
                copy_rec(t - 1)
            copy_rec(T - 1)
            for m in range(KC):
                act.wait_ge(mix_done, m + 1)
                if m >= 2:
                    act.wait_ge(mix_out, m - 1)
                for k in range(2):
                    fn(sig[:, m % 2, k, :], bank[:, 4 * (m % 2) + k, :], ACT.Sigmoid).then_inc(gate_ready, 1)
            for t in range(T):
                act.wait_ge(var_ready, t + 1)
                fn(rstd[:, :], rstd[:, :], ACT.Sqrt).then_inc(std_ready, 1)
                if t:
                    for u in (2 * t - 2, 2 * t - 1):
                        copy_x1(u)
            for u in (2 * T - 2, 2 * T - 1):
                copy_x1(u)
            for b in range(2 * PH):
                act.wait_ge(pq_done, b + 1)
                fn(qTp[:, b, :], bank[:, b % 4, :], ACT.Copy).then_inc(pq_out, 1)
            for u in range(4 * T):
                act.wait_ge(ks_done, u + 1)
                fn(s12[:, u // 4, u % 4 * 512:(u % 4 + 1) * 512], bank[:, 4 + u % 4, :], ACT.Copy).then_inc(ks_out, 1)

            with act.Fori(0, T) as t:
                act.wait_ge(gexp_arg, t + 1)
                fn(gexp[:, :, :], gexp[:, :, :], ACT.Exp).then_inc(gexp_done, 1)
                act.wait_ge(hid_ready, t + 1)
                fn(hid[:, :], hid[:, :], ACT.Gelu).then_inc(gelu_done, 1)
                act.wait_ge(wv_ready, t + 1)
                act.sem_inc(act_gate, 1)
                with act.Fori(0, ROUNDS) as i:
                    for g in range(GPR):
                        act.wait_ge(v_used, GPP * t + GPR * i + g + 1)
                        act.sem_inc(act_gate, 1)
                        for k in range(GRP):
                            s = g * GRP + k
                            last = fn(diag[:, s, :], ident[:, :], ACT.Copy, scale=wv[:, bass.ds(i * SLOTS + s, 1)])
                        last.then_inc(diag_ready, 1)
                act.wait_ge(var_ready, t + T + 1)
                fn(rstd[:, :], rstd[:, :], ACT.Sqrt).then_inc(std_ready, 1)

        @block.vector
        def _(dve):
            v = nc.vector
            ch = Chain(dve)

            def steps(*ins):
                for x in ins:
                    ch(x())
                ch.wait()

            dve.wait_ge(consts_in, 16 * (CONSTS - 2))
            steps(lambda: v.tensor_tensor(lbm[:, :], lbl[:, 0, :], lbl[:, 1, :], ALU.max),
                  lambda: v.tensor_copy(pos_f[:, :], pos_i[:, :]),
                  lambda: v.tensor_scalar(alphaI[:, :], ident[:, :], ALPHA, None, ALU.mult),
                  lambda: v.memset(AT, 0.0) if False else v.memset(mv[:, :], 0.0))
            dve.sem_inc(alpha_ready, 1)
            v.tensor_tensor(lbl[:, :, :], lbl[:, :, :], lbm.unsqueeze(1).to_broadcast([P, 2, HH]) if False else
                            lbm[:, :].unsqueeze(1).to_broadcast([P, 2, HH]), ALU.subtract).then_inc(lb_arg, 1)
            steps(lambda: v.tensor_tensor(ang[:, :, :], pos_f[:, :].unsqueeze(2).to_broadcast([P, T, HALF]),
                                          freq[:, :].unsqueeze(1).to_broadcast([P, T, HALF]), ALU.mult))
            steps(lambda: v.tensor_scalar(turns[:, :, :], ang[:, :, :], 1.0 / (2 * math.pi), None, ALU.mult))
            steps(lambda: v.tensor_scalar(turns[:, :, :], turns[:, :, :], MAGIC, None, ALU.add))
            steps(lambda: v.tensor_scalar(turns[:, :, :], turns[:, :, :], MAGIC, None, ALU.subtract))
            for part in (PI2_A, PI2_B, PI2_C):
                steps(lambda: v.scalar_tensor_tensor(out=ang[:, :, :], in0=turns[:, :, :], scalar=-part,
                                                     in1=ang[:, :, :], op0=ALU.mult, op1=ALU.add))
            steps(lambda: v.tensor_scalar(trig[:, 1, :, :], ang[:, :, :], 3.1415925, -3.1415925, ALU.min, ALU.max))
            steps(lambda: v.tensor_scalar(trig[:, 0, :, :], trig[:, 1, :, :], -1.0, None, ALU.mult))
            steps(lambda: v.tensor_tensor(trig[:, 0, :, :], trig[:, 0, :, :], trig[:, 1, :, :], ALU.min))
            steps(lambda: v.tensor_scalar(trig[:, 0, :, :], trig[:, 0, :, :], math.pi / 2, None, ALU.add))
            dve.sem_inc(trig_arg, 1)
            dve.wait_ge(lb_exp, 1)
            steps(lambda: v.tensor_tensor(lbm[:, :], lbl[:, 0, :], lbl[:, 1, :], ALU.add))
            steps(lambda: v.reciprocal(lbm[:, :], lbm[:, :]))
            steps(lambda: v.tensor_tensor(lbv[:, :], lbl[:, 0, :], lbm[:, :], ALU.mult))
            steps(lambda: v.tensor_scalar(omlb[:, :], lbv[:, :], -1.0, 1.0, ALU.mult, ALU.add))

            dve.wait_ge(trig_ready, 1)
            dve.wait_ge(proj_out, 2 * T)
            heads = tok[:, :, 0:V0].rearrange("p t (h d) -> p t h d", d=HD)
            first, second = heads[:, :, :, 0:HALF], heads[:, :, :, HALF:ROT]
            full = [P, T, HEADS + KVH, HALF]
            cos = trig[:, 0, :, :].unsqueeze(2).to_broadcast(full)
            sin = trig[:, 1, :, :].unsqueeze(2).to_broadcast(full)
            for k in range(4):
                ch(v.tensor_tensor(rot[:, k, :, :, :], (first, second, second, first)[k],
                                   (cos, sin, cos, sin)[k], ALU.mult))
            ch.wait()
            ch(v.tensor_tensor(first, rot[:, 0, :, :, :], rot[:, 1, :, :, :], ALU.subtract))
            v.tensor_tensor(second, rot[:, 2, :, :, :], rot[:, 3, :, :, :], ALU.add).then_inc(rope_done, 1)

            for t in range(T):
                for part in range(3):
                    dve.wait_ge(qk_turned, 3 * t + part + 1)
                    src = bank[0:HD, 4 + (3 * t + part) % 3, :]
                    if part < 2:
                        src = src.rearrange("p (h c q) -> p h c q", h=4, c=2)
                        dst = qT[:, 2 * t:2 * t + 2, 4 * part:4 * part + 4, :].rearrange("p c h q -> p h c q")
                    else:
                        src = src[:, 0:KVH * P].rearrange("p (h q) -> p h q", h=KVH)
                        dst = kT[:, :, t * P:(t + 1) * P]
                    v.tensor_copy(dst, src).then_inc(qk_out, 1)

            ch(v.memset(v_even[CH:P, :, :], 0.0))
            ch(v.memset(v_odd[0:CH, :, :], 0.0))
            ch(v.tensor_copy(v_even[0:CH, :, :], tok[0:CH, :, V0:I0]))
            ch(v.tensor_copy(v_odd[CH:P, :, :], tok[CH:P, :, V0:I0]))

            steps(lambda: v.memset(SC[:, 0, :, CH:P], NEG))
            for c in range(NC):
                dve.wait_ge(score_done, c + 1)
                w = P if c else CH
                v.tensor_scalar(SC[:, c, :, 0:w], bank[:, 4 + c % 4, :].rearrange("p (j k) -> p j k", j=PAIRS)[:, :, 0:w],
                                SCALE, None, ALU.mult).then_inc(score_out, 1)
            dve.wait_ge(score_out, NC)
            steps(lambda: v.tensor_reduce(mx[:, :, :], SC, AX_X, ALU.max))
            sink = sinkc[:, :].unsqueeze(1).to_broadcast([P, NC, PAIRS])
            steps(lambda: v.tensor_tensor(mx[:, :, :], mx[:, :, :], sink, ALU.max))
            wide = [P, NC, PAIRS, P]
            steps(lambda: v.tensor_tensor(SC, SC, mx[:, :, :].unsqueeze(3).to_broadcast(wide), ALU.subtract),
                  lambda: v.tensor_tensor(snk[:, :, :], sink, mx[:, :, :], ALU.subtract))
            dve.sem_inc(soft_arg, 1)
            dve.wait_ge(soft_exp, 2)
            steps(lambda: v.tensor_reduce(den[:, :, :], SC, AX_X, ALU.add))
            steps(lambda: v.tensor_tensor(den[:, :, :], den[:, :, :], snk[:, :, :], ALU.add))
            steps(lambda: v.reciprocal(den[:, :, :], den[:, :, :]))
            v.tensor_tensor(SC, SC, den[:, :, :].unsqueeze(3).to_broadcast(wide), ALU.mult).then_inc(soft_done, 1)

            for c in range(NC):
                dve.wait_ge(av_done, c + 1)
                v.tensor_copy(attnT[:, :, c * CH:(c + 1) * CH],
                              bank[:, 6 + c % 2, 0:PAIRS * CH].rearrange("p (j q) -> p j q", j=PAIRS)).then_inc(av_out, 1)

            dve.wait_ge(hgrn_act, GATES)
            for h in range(HH):
                ch(v.tensor_scalar(HF[:, h, :], HF[:, h, :], omlb[:, h:h + 1], lbv[:, h:h + 1], ALU.mult, ALU.add))
            ch.wait()
            for h in range(HH):
                v.tensor_scalar(KH[:, h, :], HF[:, h, :], -1.0, 1.0, ALU.mult, ALU.add).then_inc(fg_ready, 1)
            for h in range(HH):
                dve.wait_ge(hgrn_act, GATES + h + 1)
                ch(v.tensor_tensor_scan(BC[:, h, :], chunk_mask[:, :], HF[:, h, :], 0.0, ALU.mult, ALU.add))
            ch.wait()
            chunks = [P, HH * NC, CH]
            BCc, HFc = (z.rearrange("p h (c l) -> p (h c) l", l=CH) for z in (BC, HF))
            v.tensor_tensor(HFc, BCc[:, :, CH - 1:CH].to_broadcast(chunks), BCc, ALU.subtract).then_inc(bcum_ready, 1)
            dve.wait_ge(hgrn_act, GATES + HH + 1)
            ch(v.tensor_tensor(HQ, HQ, SQ, ALU.mult))
            ch(v.tensor_copy(decay[:, :, :], SQ.rearrange("p h (c l) -> p h c l", l=CH)[:, :, :, CH - 1]))
            dve.wait_ge(hgrn_act, GATES + HH + 2)
            ch(v.tensor_tensor(HF, HF, KH, ALU.mult))
            ch.wait()
            dve.wait_ge(hgrn_act, GATES + HH + 3)
            v.tensor_tensor(KH, KH, BC, ALU.mult).then_inc(kq_ready, 1)
            gate = tok[:, :, G0:G0 + HH * DV].rearrange("p t (h e) -> p t h e", h=HH)
            ch(v.tensor_tensor(gate, gate, normg[:, :].unsqueeze(1).unsqueeze(1).to_broadcast([P, T, HH, DV]), ALU.mult))
            ch(v.memset(ST[:, 0, :, :], 0.0))
            ch(v.memset(AT, 0.0))
            ch.wait()

            for t in range(T):
                dve.wait_ge(at_done, t + 1)
                v.copy_predicated(AT[:, t, :, :], causal[:, :].unsqueeze(1).to_broadcast([P, HH, P]),
                                  bank[:, 6 + t % 2, :].rearrange("p (h l) -> p h l", h=HH)).then_inc(at_out, 1)

            def state(c):
                dve.wait_ge(kv_done, c + 1)
                dve.wait_ge(state_ready, c + 1)
                for h in range(HH):
                    last = v.scalar_tensor_tensor(out=ST[:, c + 1, h, :], in0=ST[:, c, h, :],
                                                  scalar=decay[:, h, c:c + 1],
                                                  in1=bank[:, c % 2, h * DV:(h + 1) * DV], op0=ALU.mult, op1=ALU.add)
                last.then_inc(state_ready, 1)

            def norm_rec(t):
                dve.wait_ge(o_done, t + 1)
                o = bank[:, 2 + t % 2, :].rearrange("p (h e) -> p h e", h=HH)
                steps(lambda: v.tensor_copy(otok[:, t, :, :], o))
                steps(lambda: v.tensor_tensor(osq, otok[:, t, :, :], otok[:, t, :, :], ALU.mult))
                steps(lambda: v.tensor_reduce(rms[:, t, :], osq, AX_X, ALU.add))
                v.tensor_scalar(rms[:, t, :], rms[:, t, :], 1.0 / DV, RMS_EPS, ALU.mult, ALU.add).then_inc(ms_ready, 1)
                dve.wait_ge(rms_root, t + 1)
                steps(lambda: v.reciprocal(rms[:, t, :], rms[:, t, :]))
                steps(lambda: v.tensor_tensor(otok[:, t, :, :], otok[:, t, :, :],
                                              rms[:, t, :].unsqueeze(2).to_broadcast([P, HH, DV]), ALU.mult))
                v.tensor_tensor(otok[:, t, :, :], otok[:, t, :, :],
                                tok[:, t, G0:G0 + HH * DV].rearrange("p (h e) -> p h e", h=HH),
                                ALU.mult).then_inc(rec_ready, 1)

            dve.sem_inc(state_ready, 1)
            state(0)
            for t in range(T):
                for c in (2 * t + 1, 2 * t + 2):
                    if c < NC - 1:
                        state(c)
                norm_rec(t)

            for m in range(KC):
                b = 4 * (m % 2)
                dve.wait_ge(gate_ready, 2 * m + 2)
                for k in range(2):
                    ch(v.tensor_tensor(sig[:, m % 2, k, :], sig[:, m % 2, k, :], bank[:, b + 2 + k, :], ALU.mult))
                ch.wait()
                v.tensor_tensor(mixT[:, m, :], sig[:, m % 2, 0, :], sig[:, m % 2, 1, :], ALU.add).then_inc(mix_out, 1)

            def layer_norm(t, src, dst, gb, ready, read=None):
                for n in range(2):
                    ch(v.bn_stats(stats[:, n, :], src[:, n * 512:(n + 1) * 512]))
                ch.gate()
                steps(lambda: v.bn_aggr(mv[:, :], stats[:, :, :]))
                v.tensor_scalar(rstd[:, :], mv[:, 1:2], LN_EPS, None, ALU.add).then_inc(var_ready, 1)
                dve.wait_ge(std_ready, t + 1)
                steps(lambda: v.reciprocal(rstd[:, :], rstd[:, :]))
                ch(v.tensor_scalar(dst, src, mv[:, 0:1], rstd[:, 0:1], ALU.subtract, ALU.mult))
                ch.wait()
                if read is not None:
                    dve.sem_inc(read, 1)
                steps(lambda: v.tensor_tensor(dst, dst, gb[:, 0, :], ALU.mult))
                v.tensor_tensor(dst, dst, gb[:, 1, :], ALU.add).then_inc(ready, 1)

            dve.wait_ge(x_in, 16)
            dve.wait_ge(ln1_in, 32)
            for t in range(T):
                for n in range(2):
                    u = 2 * t + n
                    dve.wait_ge(y_done, u + 1)
                    xs = x1[:, t, n * 512:(n + 1) * 512]
                    v.scalar_tensor_tensor(out=xs, in0=xs, scalar=ALPHA, in1=bank[:, u % 4, :],
                                           op0=ALU.mult, op1=ALU.add).then_inc(y_out, 1)
                dve.wait_ge(y_out, 2 * t + 2)
                layer_norm(t, x1[:, t, :], x1[:, t, :], ln_gb, x1_ready)

            eidx_all = eidx[:, :, :].rearrange("p t e -> p (t e)")
            s12_all = s12.rearrange("p t s -> p (t s)")
            x1_all = x1[:, :, :].rearrange("p t d -> p (t d)")

            def top16(values, best, index, n):
                for half in range(2):
                    part = slice(8 * half, 8 * half + 8)
                    for b in range(n):
                        ch(v.max(best(b)[:, part], values(b)))
                    ch.gate()
                    for b in range(n):
                        ch(v.max_index(index(b)[:, part], best(b)[:, part], values(b)))
                    ch.gate()
                    if half == 0:
                        for b in range(n):
                            ch(v.match_replace(values(b), best(b)[:, part], values(b), LOWEST))
                        ch.gate()

            def route(t):
                ch.gate()
                ch(v.tensor_copy(scur.rearrange("p b k -> p (b k)"),
                                 s12_all[:, bass.ds(t * (2 * PH * NK), 2 * PH * NK)]))
                ch.gate()
                top16(lambda b: scur[:, b, :], lambda b: top[:, b // 2, b % 2, :],
                      lambda b: topi[:, b // 2, b % 2, :], 2 * PH)
                sums = [P, PH, TOPK, TOPK]
                steps(lambda: v.tensor_copy(topf[:, :, :, :], topi[:, :, :, :]),
                      lambda: v.tensor_tensor(cand, top[:, :, 0, :].unsqueeze(3).to_broadcast(sums),
                                              top[:, :, 1, :].unsqueeze(2).to_broadcast(sums), ALU.add))
                ch.gate()
                top16(lambda h: cand[:, h, :, :].rearrange("p i j -> p (i j)"), lambda h: sco[:, h, :],
                      lambda h: sci[:, h, :], PH)
                v.tensor_tensor(gexp[:, :, :], sco[:, :, :], sco[:, :, 0:1].to_broadcast([P, PH, TOPK]),
                                ALU.subtract).then_inc(gexp_arg, 1)
                for half, e in ((0, e1), (1, e2)):
                    if half == 0:
                        steps(lambda: v.tensor_scalar(half_i[:, :, :], sci[:, :, :], 4, None, ALU.logical_shift_right))
                    else:
                        steps(lambda: v.tensor_scalar(half_i[:, :, :], sci[:, :, :], 15, None, ALU.bitwise_and))
                    steps(lambda: v.tensor_copy(half_f[:, :, :], half_i[:, :, :]))
                    oh = onehot.rearrange("p (h k) j -> p h k j", h=PH)
                    pk = picked.rearrange("p (h k) j -> p h k j", h=PH)
                    ranks = half_f[:, :, :].rearrange("p h k -> p (h k)").unsqueeze(2).to_broadcast([P, NE, TOPK])
                    steps(lambda: v.tensor_tensor(onehot, ranks, iota16[:, :].unsqueeze(1).to_broadcast([P, NE, TOPK]),
                                                  ALU.is_equal))
                    steps(lambda: v.tensor_tensor(pk, oh, topf[:, :, half, :].unsqueeze(2).to_broadcast(sums), ALU.mult))
                    steps(lambda: v.tensor_reduce(e[:, :], picked, AX_X, ALU.add))
                steps(lambda: v.scalar_tensor_tensor(out=e1[:, :], in0=e1[:, :], scalar=float(NK), in1=e2[:, :],
                                                     op0=ALU.mult, op1=ALU.add))
                ch.gate()
                v.tensor_copy(eidx_all[:, bass.ds(t * NE, NE)], e1[:, :]).then_inc(idx_ready, 1)

            def hidden(t, times_in):
                ch.gate()
                ch(v.tensor_copy(x1cur, x1_all[:, bass.ds(t * D, D)]))
                with dve.Fori(0, ROUNDS) as i:
                    ch.enter(i, 1)
                    for s in range(SLOTS):
                        if s == 0:
                            ch.wait()
                        dve.wait_ge(landed[s], 16 * (2 * ROUNDS * t + i + 1))
                        last = v.tensor_tensor_reduce(rows[:, s, :], rows[:, s, :], x1cur, 1.0, 0.0,
                                                      ALU.mult, ALU.add, hid_r[:, s:s + 1])
                        if s % GRP == GRP - 1:
                            last.then_inc(u_used, 1)
                    dve.wait_ge(u_used, GPP * t + GPR * i + GPR)
                    dve.sem_inc(route_gate, 1)
                    ch(v.tensor_copy(hid[:, bass.ds(i * SLOTS, SLOTS)], hid_r[:, :]))
                    ch.leave(ROUNDS)
                ch.wait()
                dve.sem_inc(hid_ready, 1)

            def weights(t):
                dve.wait_ge(gexp_done, t + 1)
                steps(lambda: v.tensor_reduce(gsum[:, :], gexp[:, :, :], AX_X, ALU.add))
                steps(lambda: v.reciprocal(gsum[:, :], gsum[:, :]))
                steps(lambda: v.tensor_tensor(gexp[:, :, :], gexp[:, :, :],
                                              gsum[:, :].unsqueeze(2).to_broadcast([P, PH, TOPK]), ALU.mult))
                dve.wait_ge(gelu_done, t + 1)
                v.tensor_tensor(wv[:, :], hid[:, :], gexp[:, :, :].rearrange("p h k -> p (h k)"),
                                ALU.mult).then_inc(wv_ready, 1)
                dve.wait_ge(wv_ready, t + 1)

            def second_norm(t):
                dve.wait_ge(v_used, GPP * (t + 1) + GPR)
                dve.wait_ge(y_free, t + 1)
                dve.sem_inc(route_gate, 1)
                acc = bank[:, 0:2, :].rearrange("p b n -> p (b n)")
                layer_norm(t + T, acc, ybuf, ln_gb, y2_ready, read=acc_out)
                dve.wait_ge(y2_ready, t + 1)

            dve.wait_ge(ks_out, 4 * T)
            dve.wait_ge(ln2_in, 32)
            route(0)
            with dve.Fori(0, T - 1) as t:
                ch.enter(t, PER_TILE)
                hidden(t, T - 1)
                weights(t)
                route(t + 1)
                second_norm(t)
                ch.leave(T - 1)
            hidden(T - 1, 1)
            weights(T - 1)
            second_norm(T - 1)

        @block.gpsimd
        def _(pool):
            pool.sem_inc(v_used, GPR)
            pool.sem_inc(acc_out, 1)
            eidx_all = eidx[:, :, :].rearrange("p t e -> p (t e)")

            def gather(t, table, phase, i, g, free, count):
                pool.wait_ge(free, count)
                pool.sem_inc(pool_gate, 1)
                sl = slice(g * GRP, (g + 1) * GRP)
                nc.gpsimd.tensor_copy(cur[:, sl], eidx_all[:, bass.ds(t * NE + i * SLOTS + g * GRP, GRP)]).then_inc(cur_ready, 1)
                pool.wait_ge(cur_ready, 2 * GPP * t + GPP * phase + GPR * i + g + 1)
                pool.sem_inc(pool_gate, 1)
                for s in range(g * GRP, (g + 1) * GRP):
                    pool.indirect_dma_start(rows[:, s, :], None, table,
                                            bass.IndirectOffsetOnAxis(cur[:, s:s + 1], 0)).then_inc(landed[s], 16)

            with pool.Fori(0, T) as t:
                pool.wait_ge(idx_ready, t + 1)
                for phase, table, used, credit in ((0, u_rows, u_used, 0), (1, v_rows, v_used, GPR)):
                    for g in range(GPR):
                        if phase == 0:
                            gather(t, table, phase, 0, g, v_used, GPP * t + g + 1)
                        else:
                            gather(t, table, phase, 0, g, u_used, GPP * t + GPP - GPR + g + 1)
                    with pool.Fori(1, ROUNDS) as i:
                        for g in range(GPR):
                            gather(t, table, phase, i, g, used, credit + GPP * t + GPR * (i - 1) + g + 1)


def kernel(**inputs):
    import numpy as np
    import concourse.bacc as bacc
    from concourse.bass_utils import run_bass_kernel_spmd

    nc = bacc.Bacc("TRN2", target_bir_lowering=False, num_devices=1)
    arrays = {}

    def dram(name, a):
        a = np.ascontiguousarray(a)
        arrays[name] = a
        return nc.dram_tensor(name, a.shape, mybir.dt.from_np(a.dtype), kind="ExternalInput").ap()

    def get(name):
        return np.asarray(inputs[name])

    def blocks(w, n):
        return w.reshape(w.shape[0] // P, P, n, w.shape[1] // n).transpose(2, 1, 0, 3).reshape(n, P, -1)

    x = get("x")[0]
    w_in = get("w_in")[0]
    widths = (HEADS * HD, KVH * HD, KVH * HD, HH * DK, HH * DK, HH * DV, HH * DV, D, D)
    q, k, v, hq, hf, hi, hg, ga, gh = np.split(w_in, np.cumsum(widths)[:-1], axis=1)
    mix = np.concatenate([blocks(get(n)[0] if isinstance(n, str) else n, KC)
                          for n in (ga, gh, "w_proj_attn", "w_proj_hgrn")], axis=2)
    causal = np.kron(np.eye(2, dtype=np.uint32), np.triu(np.ones((CH, CH), np.uint32)))
    chunk = np.tile((np.arange(S) % CH != 0).astype(np.float32), (P, 1))
    freq = (np.float32(500000.0) ** (-np.arange(0, ROT, 2, dtype=np.float32) / np.float32(ROT))).astype(np.float32)
    args = [
        dram("x_d", x), dram("xT_d", x.T),
        dram("w_tok_d", blocks(np.concatenate([q, k, v, hi, hg], axis=1), TG)),
        dram("w_hqf_d", blocks(np.concatenate([hq, hf], axis=1), 2)),
        dram("w_mix_d", mix),
        dram("w_out_d", blocks(get("w_out")[0], 2)),
        dram("w_q_d", blocks(get("peer_wq")[0], 4)),
        dram("keysT_d", get("peer_keys")[0].transpose(2, 0, 1)),
        dram("pos_d", get("positions")[0].reshape(T, P).T),
        dram("freq_d", freq),
        dram("sinks_d", get("attn_sinks")[0].reshape(PAIRS, 2).T),
        dram("lb_d", get("hgrn_lb").reshape(2, HH, DK).transpose(2, 0, 1)),
        dram("norm_g_d", get("hgrn_norm_g")[0]),
        dram("ln1_d", np.stack([get("ln1_g")[0], get("ln1_b")[0]])),
        dram("ln2_d", np.stack([get("ln2_g")[0], get("ln2_b")[0]])),
        dram("ident_d", np.eye(P, dtype=np.float32)), dram("causal_d", causal), dram("chunk_d", chunk),
        dram("iota_d", np.tile(np.arange(TOPK, dtype=np.float32), (P, 1))),
        dram("u_d", get("peer_u")[0]), dram("v_d", get("peer_v")[0]),
    ]
    out = nc.dram_tensor("out_d", (S, D), F32, kind="ExternalOutput").ap()
    build(nc, *args, out)
    r = run_bass_kernel_spmd(nc, [arrays], core_ids=[0])
    return r.results[0]["out_d"].reshape(1, S, D)
```

```python
import math
from contextlib import ExitStack

import concourse.bass as bass
from concourse import mybir

P = 128
F32 = mybir.dt.float32
U32 = mybir.dt.uint32
I32 = mybir.dt.int32
ALU = mybir.AluOpType
ACT = mybir.ActivationFunctionType
AX_X = mybir.AxisListType.X

S, D = 512, 1024
T = S // P
KC = D // P
CH = 64
NC = S // CH
HEADS, KVH, HD = 8, 2, 64
PAIRS = HEADS // 2
ROT = HD // 4
HALF = ROT // 2
HH, DK, DV = 4, 128, 128
TOKW = HEADS * HD + 2 * KVH * HD + 2 * HH * DV
K0 = HEADS * HD
V0 = K0 + KVH * HD
I0 = V0 + KVH * HD
G0 = I0 + HH * DV
PH, NK, TOPK = 8, 128, 16
NE = PH * TOPK
SCALE = 1.0 / math.sqrt(HD)
NEG = -1e30
LOWEST = -3.0e38
PER_TILE = 178
ALPHA = 2.0 ** 0.25
LN_EPS = 1e-5
RMS_EPS = 1e-6

RING, ITEMW = 3, 2048
TW = 256
N_HQF, N_TOK, N_MIX, N_OUT, N_WQ = 4, TOKW // TW, 3 * KC // 2, D // TW, PH
TOK_EARLY = 5
I_TOK = N_HQF
I_MIX = I_TOK + N_TOK
I_OUT = I_MIX + N_MIX
I_WQ = I_OUT + N_OUT
ITEMS = I_WQ + N_WQ

SLOTS, GRP = 16, 4
GPR = SLOTS // GRP
ROUNDS = NE // SLOTS
GPP = GPR * ROUNDS
SHARE_FROM = 2
EARLY_V = 6
PER_TILE = 178

AT_FG, AT_ROPE, AT_HGRN, AT_SOFT, AT_SOFT2, AT_CAUSAL, AT_REC, AT_MIX, MIX_STEP = 40, 44, 46, 52, 54, 60, 66, 78, 7
AT_OUT, OUT_STEP, AT_LN, LN_STEP = 130, 4, 150, 6
ROUTE_ROWS = 4
assert AT_MIX + 7 * MIX_STEP <= NE < AT_LN

PI2_A = 6.28125
PI2_B = math.floor((2 * math.pi - PI2_A) * 2 ** 19) / 2 ** 19
PI2_C = 2 * math.pi - PI2_A - PI2_B
MAGIC = 1.5 * 2 ** 23


class Front:

    def __init__(self, name, t0, nt, item0, sem):
        self.name, self.t0, self.nt, self.item0 = name, t0, nt, item0
        self.n, self.nc = nt * P, 2 * nt
        self.xT_in = sem(f"{name}_xT_in")
        self.x_in = sem(f"{name}_x_in")
        self.proj_done = sem(f"{name}_proj_done")
        self.proj_out = sem(f"{name}_proj_out")
        self.rope_done = sem(f"{name}_rope_done")
        self.qk_turned = sem(f"{name}_qk_turned")
        self.qk_out = sem(f"{name}_qk_out")
        self.score_done = sem(f"{name}_score_done")
        self.score_out = sem(f"{name}_score_out")
        self.soft_arg = sem(f"{name}_soft_arg")
        self.soft_exp = sem(f"{name}_soft_exp")
        self.soft_done = sem(f"{name}_soft_done")
        self.w_turned = sem(f"{name}_w_turned")
        self.w_outT = sem(f"{name}_w_outT")
        self.av_done = sem(f"{name}_av_done")
        self.av_out = sem(f"{name}_av_out")
        self.hgrn_ln = sem(f"{name}_hgrn_ln")
        self.fg_ready = sem(f"{name}_fg_ready")
        self.bcum_ready = sem(f"{name}_bcum_ready")
        self.hgrn_exp = sem(f"{name}_hgrn_exp")
        self.kq_ready = sem(f"{name}_kq_ready")
        self.vz_ready = sem(f"{name}_vz_ready")
        self.kend_turned = sem(f"{name}_kend_turned")
        self.kend_out = sem(f"{name}_kend_out")
        self.at_done = sem(f"{name}_at_done")
        self.at_out = sem(f"{name}_at_out")
        self.kv_done = sem(f"{name}_kv_done")
        self.state_ready = sem(f"{name}_state_ready")
        self.o_done = sem(f"{name}_o_done")
        self.ms_ready = sem(f"{name}_ms_ready")
        self.rms_root = sem(f"{name}_rms_root")
        self.rec_ready = sem(f"{name}_rec_ready")
        self.rec_turned = sem(f"{name}_rec_turned")
        self.rec_out = sem(f"{name}_rec_out")
        self.gate_done = sem(f"{name}_gate_done")
        self.gate_ready = sem(f"{name}_gate_ready")
        self.mix_done = sem(f"{name}_mix_done")
        self.mix_out = sem(f"{name}_mix_out")
        self.y_done = sem(f"{name}_y_done")
        self.y_out = sem(f"{name}_y_out")
        self.var_ready = sem(f"{name}_var_ready")
        self.std_ready = sem(f"{name}_std_ready")
        self.x1_ready = sem(f"{name}_x1_ready")
        self.x1_turned = sem(f"{name}_x1_turned")
        self.x1_out = sem(f"{name}_x1_out")
        self.pq_done = sem(f"{name}_pq_done")
        self.pq_out = sem(f"{name}_pq_out")
        self.ks_done = sem(f"{name}_ks_done")
        self.ks_out = sem(f"{name}_ks_out")


def build(nc, x, xT, w_items, keysT, pos, inv_freq, sinks, lb_logits, norm_g,
          ln1, ln2, ident_d, causal_d, chunk_d, iota_d, u_rows, v_rows, out):
    with ExitStack() as ctx:
        def sb(name, shape, dt=F32):
            return ctx.enter_context(nc.sbuf_tensor(name, shape, dt))

        def sem(name):
            return ctx.enter_context(nc.semaphore(name))

        KB = 256
        arena = sb("arena", [P, 198 * KB])

        def view(kb, *dims, parts=P, dt=F32):
            n = 1
            for d in dims:
                n *= d
            a = arena[0:parts, int(kb * KB):int(kb * KB) + n]
            if dt != F32:
                a = a.bitcast(dt)
            if len(dims) == 1:
                return a
            names = "abcd"[:len(dims)]
            return a.rearrange(f"p ({' '.join(names)}) -> p {' '.join(names)}",
                               **{k: d for k, d in zip(names[1:], dims[1:])})

        rows = view(0, SLOTS, D)
        ring = view(64, RING, ITEMW)
        x1 = view(88, T, D)
        ln_gb = view(182, 2, D)
        acc = view(190, D)
        cur = view(194, SLOTS, dt=U32)
        eidx = view(194.125, T, NE, dt=U32)
        gexp = view(196.125, PH, TOPK)
        hid = view(196.625, NE)
        wv = view(197.125, NE)
        hid_r = view(197.625, SLOTS)
        gsum = view(197.75, PH)
        top = view(176, PH, 2, TOPK)
        topi = view(177, PH, 2, TOPK, dt=U32)
        topf = view(178, PH, 2, TOPK)
        sco = view(179, PH, TOPK)
        sci = view(179.5, PH, TOPK, dt=U32)
        half_i = view(180, PH, TOPK, dt=U32)
        half_f = view(180.5, PH, TOPK)
        e1 = view(181, NE)
        e2 = view(181.5, NE)
        ybuf = view(104, D)
        x1cur = view(108, D)
        diag = view(112, SLOTS, P)
        scur = view(120, 2 * PH, NK)
        cand = view(128, PH, TOPK, TOPK)
        onehot = view(164, NE, TOPK)
        picked = view(172, 2, TOPK, TOPK)
        cand0, onehot0, picked0 = view(172, TOPK, TOPK), view(173, TOPK, TOPK), view(174, TOPK, TOPK)

        ident = sb("ident", [P, P])
        alphaI = sb("alphaI", [P, P])
        causal = sb("causal", [P, P], U32)
        chunk_mask = sb("chunk_mask", [P, (T - 1) * P])
        iota16 = sb("iota16", [P, TOPK])
        keys = sb("keys", [P, 2, NK])
        normg = sb("normg", [P, DV])
        state_in = sb("state_in", [P, HH, DV])
        k_last = sb("k_last", [HD, KVH, CH])
        v_last = sb("v_last", [P, KVH * HD])
        pos_i = sb("pos_i", [P, T], I32)
        pos_f = sb("pos_f", [P, T])
        freq = sb("freq", [P, HALF])
        sinkc = sb("sinkc", [P, PAIRS])
        lbl = sb("lbl", [P, 2, HH])
        lbm = sb("lbm", [P, HH])
        lbv = sb("lbv", [P, HH])
        omlb = sb("omlb", [P, HH])
        ang = sb("ang", [P, T, HALF])
        turns = sb("turns", [P, T, HALF])
        trig = sb("trig", [P, 2, T, HALF])
        mxb = sb("mx", [P, 3, NC, PAIRS])
        decayb = sb("decay", [P, HH, NC])
        rmsb = sb("rms", [P, T, HH])
        stats = sb("stats", [P, 2, 6])
        mv = sb("mv", [P, 2])
        rstd = sb("rstd", [P, 1])
        bank = ctx.enter_context(nc.psum_tensor("bank", [P, 8, 512], F32))

        A = Front("a", 0, 1, 0, sem)
        B = Front("b", 1, T - 1, ITEMS, sem)
        consts_in = sem("consts_in")
        ln1_in = sem("ln1_in")
        ln2_in = sem("ln2_in")
        w_in = [sem(f"w_in{i}") for i in range(RING)]
        trig_arg = sem("trig_arg")
        trig_ready = sem("trig_ready")
        lb_arg = sem("lb_arg")
        lb_exp = sem("lb_exp")
        alpha_ready = sem("alpha_ready")
        step = sem("step")
        route_gate = sem("route_gate")
        idx_ready = sem("idx_ready")
        gexp_arg = sem("gexp_arg")
        gexp_done = sem("gexp_done")
        cur_ready = sem("cur_ready")
        pool_gate = sem("pool_gate")
        landed = [sem(f"landed{i}") for i in range(SLOTS)]
        u_used = sem("u_used")
        v_used = sem("v_used")
        v_shared = sem("v_shared")
        hid_ready = sem("hid_ready")
        gelu_done = sem("gelu_done")
        wv_ready = sem("wv_ready")
        act_gate = sem("act_gate")
        diag_ready = sem("diag_ready")
        acc_out = sem("acc_out")
        var2_ready = sem("var2_ready")
        std2_ready = sem("std2_ready")
        y2_ready = sem("y2_ready")
        y_free = sem("y_free")
        out_done = sem("out_done")

        A.tok = view(0, 1, TOKW)
        A.HQ, A.HF, A.KH = (view(7 + 2 * k, HH, A.n) for k in range(3))
        A.SQ, A.BC = view(13, 2, A.n), view(14, 2, A.n)
        A.rot = view(15, 4, 1, HEADS + KVH, HALF)
        A.qT = view(17, A.nc, HEADS, CH, parts=HD)
        A.SC = view(21, A.nc, PAIRS, P)
        A.PT = view(25, A.nc, PAIRS, P)
        A.attnT, A.recT = view(29, PAIRS, A.n), view(31, HH, A.n)
        A.kendT, A.AT, A.otok = view(33, 1, HH, DK), view(35, 1, HH, P), view(37, 1, HH, DV)
        A.ST = [view(39, HH, DV), view(41, HH, DV), state_in[:, :, :]]
        A.mixT = view(43, KC, A.n)
        A.sig = view(47, 2, 2, A.n)
        A.osq = view(49, HH, DV)
        A.act_in = view(190, KC, A.n)
        A.qTp = view(140, 2 * PH, A.n)
        A.s12 = view(164, 1, 2 * PH * NK)
        B.HQ, B.HF = view(92, HH, B.n), view(98, HH, B.n)
        B.act_in = view(104, KC, B.n)
        B.tok = view(116, B.nt, TOKW)
        B.qTp = view(116, 2 * PH, B.n)
        B.rot = view(140, 4, B.nt, HEADS + KVH, HALF)
        B.qT = view(140, B.nc, HEADS, CH, parts=HD)
        B.PT = view(140, B.nc, PAIRS, P)
        B.SC = view(152, B.nc, PAIRS, P)
        B.attnT = view(164, PAIRS, B.n)
        B.KH = view(170, HH, B.n)
        B.SQ, B.BC = view(176, 2, B.n), view(179, 2, B.n)
        B.kendT, B.AT = view(140, B.nt, HH, DK), view(146, B.nt, HH, P)
        B.ST = [state_in[:, :, :]] + [view(150 + 2 * k, HH, DV) for k in range(1, B.nc)]
        B.otok = view(98, B.nt, HH, DV)
        B.osq = view(179, HH, DV)
        B.recT = view(170, HH, B.n)
        B.mixT = view(140, KC, B.n)
        B.sig = view(152, 2, 2, B.n)
        B.s12 = view(140, B.nt, 2 * PH * NK)
        for F in (A, B):
            F.mx, F.snk, F.den = (mxb[:, k, 2 * F.t0:2 * F.t0 + F.nc, :] for k in range(3))
            F.decay = decayb[:, :, 2 * F.t0:2 * F.t0 + F.nc]
            F.rms = rmsb[:, F.t0:F.t0 + F.nt, :]
            F.x1 = x1[:, F.t0:F.t0 + F.nt, :]
            F.kT = F.tok[0:HD, :, K0 - KVH * P:K0].rearrange("p t (g k) -> p t g k", g=KVH)
            F.v_even, F.v_odd = F.tok[:, :, 0:KVH * HD], F.tok[:, :, KVH * HD:2 * KVH * HD]

        CONSTS = 11

        def item(F, k):
            return ring[:, (F.item0 + k) % RING, :]

        def item_in(eng, F, k):
            n = F.item0 + k
            eng.wait_ge(w_in[n % RING], 16 * (n // RING + 1))

        def item_used(eng, F, k):
            if k < I_TOK:
                eng.wait_ge(F.proj_done, 2 * (k + 1))
            elif k < I_MIX:
                eng.wait_ge(F.proj_done, 2 * N_HQF + F.nt * (k - I_TOK + 1))
            elif k < I_OUT:
                pair, part = (k - I_MIX) // 3, (k - I_MIX) % 3
                if part < 2:
                    eng.wait_ge(F.gate_done, 2 * pair + part + 1)
                else:
                    eng.wait_ge(F.mix_done, 2 * pair + 2)
            elif k < I_WQ:
                eng.wait_ge(F.y_done, F.nt * (k - I_OUT + 1))
            else:
                eng.wait_ge(F.pq_done, 2 * (k - I_WQ + 1))

        class Chain:

            def __init__(self, eng):
                self.eng, self.n, self.dyn = eng, 0, []

            def value(self):
                v = self.n
                for turn, per in self.dyn:
                    v = turn * per + v
                return v

            def __call__(self, ins):
                ins.then_inc(step, 1)
                self.n += 1
                return ins

            def wait(self):
                self.eng.wait_ge(step, self.value())

            def gate(self):
                self.wait()
                self.eng.sem_inc(route_gate, 1)

            def enter(self, turn, per):
                self.dyn.append((turn, per))
                self.start = (self.n, per)

            def leave(self, start, times):
                _, per = self.dyn.pop()
                assert self.n - start == per, (self.n - start, per)
                self.n = start + per * times

        block = ctx.enter_context(nc.Block())

        @block.sync
        def _(sp):
            def load(F, k):
                n = F.item0 + k
                if n >= RING:
                    old = n - RING
                    item_used(sp, *((A, old) if old < ITEMS else (B, old - ITEMS)))
                sp.dma_start(item(F, k), w_items[k]).then_inc(w_in[n % RING], 16)

            def load_xT(F):
                sp.dma_start(F.act_in, xT.rearrange("(c p) t -> p c t", p=P)[:, :, F.t0 * P:(F.t0 + F.nt) * P]
                             ).then_inc(F.xT_in, 16)

            def load_x(F):
                sp.dma_start(F.x1, x.rearrange("(t p) d -> p t d", p=P)[:, F.t0:F.t0 + F.nt, :]).then_inc(F.x_in, 16)

            load_xT(A)
            load(A, 0)
            load(A, 1)
            for dst, src in ((ident[:, :], ident_d), (causal[:, :], causal_d), (chunk_mask[:, :], chunk_d),
                             (iota16[:, :], iota_d), (keys[:, :, :], keysT), (pos_i[:, :], pos),
                             (lbl[:, :, :], lb_logits), (freq[:, :], inv_freq.partition_broadcast(P)),
                             (normg[:, :], norm_g.partition_broadcast(P))):
                sp.dma_start(dst, src).then_inc(consts_in, 16)
            for hh in range(2):
                sp.dma_start(sinkc[CH * hh:CH * hh + CH, :], sinks[hh, :].partition_broadcast(CH)).then_inc(consts_in, 16)
            for k in range(2, 8):
                load(A, k)
            load_x(A)
            load_xT(B)
            for k in range(2):
                sp.dma_start(ln_gb[:, k, :], ln1[k, :].partition_broadcast(P)).then_inc(ln1_in, 16)
            for k in range(8, ITEMS):
                load(A, k)
            for k in range(ITEMS):
                load(B, k)
                if k == I_MIX + RING:
                    sp.wait_ge(B.rec_turned, B.nt)
                    load_x(B)
            sp.wait_ge(B.x1_ready, B.nt)
            for k in range(2):
                sp.dma_start(ln_gb[:, k, :], ln2[k, :].partition_broadcast(P)).then_inc(ln2_in, 16)
            sp.sem_inc(y_free, 1)
            with sp.Fori(0, T) as t:
                sp.wait_ge(y2_ready, t + 1)
                sp.dma_start(out[bass.ds(t * P, P), :], ybuf).then_inc(out_done, 16)
                sp.wait_ge(out_done, 16 * (t + 1))
                sp.sem_inc(y_free, 1)
            sp.wait_ge(out_done, 16 * T)

        @block.tensor
        def _(pe):
            mm = nc.tensor.matmul
            turn = nc.tensor.transpose

            def front(F, other=None):
                n, nt = F.n, F.nt
                pe.wait_ge(F.xT_in, 16)
                if other is not None:
                    pe.wait_ge(other.pq_out, 2 * PH)

                for b in range(2 * N_HQF):
                    item_in(pe, F, b // 2)
                    w = item(F, b // 2).rearrange("p (c n) -> p c n", c=KC)
                    if b >= 4:
                        pe.wait_ge(F.proj_out, b - 3)
                    for c in range(KC):
                        last = mm(bank[:, b % 4, 0:n], w[:, c, b % 2 * P:(b % 2 + 1) * P], F.act_in[:, c, :],
                                  start=c == 0, stop=c == KC - 1)
                    last.then_inc(F.proj_done, 1)

                def project_tok(k):
                    item_in(pe, F, I_TOK + k)
                    w = item(F, I_TOK + k).rearrange("p (c n) -> p c n", c=KC)
                    for t in range(nt):
                        b = 2 * N_HQF + k * nt + t
                        pe.wait_ge(F.proj_out, b - 3)
                        for c in range(KC):
                            last = mm(bank[:, b % 4, 0:TW], F.act_in[:, c, t * P:(t + 1) * P], w[:, c, :],
                                      start=c == 0, stop=c == KC - 1)
                        last.then_inc(F.proj_done, 1)

                for k in range(TOK_EARLY):
                    project_tok(k)

                pe.wait_ge(consts_in, 16 * CONSTS)
                pe.wait_ge(F.rope_done, 1)
                if other is not None:
                    pe.wait_ge(other.ks_out, PH)
                for t in range(nt):
                    for part in range(3):
                        u = 3 * t + part
                        if u >= 4:
                            pe.wait_ge(F.qk_out, u - 3)
                        for k in range(4 if part < 2 else 2):
                            h = 4 * part + k
                            last = turn(bank[0:HD, 4 + u % 4, k * P:(k + 1) * P],
                                        F.tok[:, t, h * HD:(h + 1) * HD], ident[:, :])
                        last.then_inc(F.qk_turned, 1)

                pe.wait_ge(F.qk_out, 3 * nt)
                for c in range(F.nc):
                    if c >= 4:
                        pe.wait_ge(F.score_out, c - 3)
                    for j in range(PAIRS):
                        g = j // (PAIRS // KVH)
                        q = F.qT[:, c, 2 * j:2 * j + 2, :]
                        o = bank[:, 4 + c % 4, j * P:(j + 1) * P]
                        if c % 2:
                            last = mm(o, q, F.kT[:, c // 2, g, :], start=True, stop=True)
                        else:
                            last = mm(o[:, 0:CH], q, F.kT[:, c // 2, g, 0:CH], start=True, stop=True)
                            if c or F.t0:
                                before = F.kT[:, c // 2 - 1, g, CH:P] if c else k_last[:, g, :]
                                last = mm(o[:, CH:P], q, before, start=True, stop=True)
                    last.then_inc(F.score_done, 1)

                for k in range(TOK_EARLY, N_TOK):
                    project_tok(k)

                def turn_weights(c):
                    if c >= 2:
                        pe.wait_ge(F.w_outT, c - 1)
                    for j in range(PAIRS):
                        last = turn(bank[:, 4 + c % 2, j * P:(j + 1) * P], F.SC[:, c, j, :], ident[:, :])
                    last.then_inc(F.w_turned, 1)

                def times_v(c):
                    pe.wait_ge(F.w_outT, c + 1)
                    if c >= 2:
                        pe.wait_ge(F.av_out, c - 1)
                    for j in range(PAIRS):
                        g = j // (PAIRS // KVH)
                        vc = slice(V0 + g * HD, V0 + (g + 1) * HD)
                        vz = slice(g * HD, (g + 1) * HD)
                        for hh in range(2):
                            o = bank[hh * HD:(hh + 1) * HD, 6 + c % 2, j * CH:(j + 1) * CH]
                            p = F.PT[:, c, j, hh * CH:(hh + 1) * CH]
                            if c % 2:
                                last = mm(o, F.tok[:, c // 2, vc], p, start=True, stop=True)
                            else:
                                first = c == 0 and F.t0 == 0
                                last = mm(o, F.v_even[:, c // 2, vz], p, start=True, stop=first)
                                if not first:
                                    before = F.v_odd[:, c // 2 - 1, vz] if c else v_last[:, vz]
                                    last = mm(o, before, p, start=False, stop=True)
                    last.then_inc(F.av_done, 1)

                pe.wait_ge(F.soft_done, 1)
                pe.wait_ge(F.vz_ready, 1)
                turn_weights(0)
                for c in range(F.nc):
                    if c + 1 < F.nc:
                        turn_weights(c + 1)
                    times_v(c)

                pe.wait_ge(F.kq_ready, 1)
                pe.wait_ge(F.av_out, F.nc)
                for t in range(nt):
                    tokens = slice(t * P, (t + 1) * P)
                    if t >= 2:
                        pe.wait_ge(F.kend_out, t - 1)
                    for h in range(HH):
                        last = turn(bank[:, 4 + t % 2, h * P:(h + 1) * P], F.HF[:, h, tokens], ident[:, :])
                    last.then_inc(F.kend_turned, 1)
                    if t >= 2:
                        pe.wait_ge(F.at_out, t - 1)
                    for h in range(HH):
                        last = mm(bank[:, 6 + t % 2, h * P:(h + 1) * P], F.KH[:, h, tokens], F.HQ[:, h, tokens],
                                  start=True, stop=True)
                    last.then_inc(F.at_done, 1)

                states = F.nc if F.t0 == 0 else F.nc - 1

                def chunk_kv(c):
                    if c >= states:
                        return
                    t, cc = c // 2, c % 2
                    pe.wait_ge(F.kend_out, t + 1)
                    if c >= 2:
                        pe.wait_ge(F.state_ready, c)
                    for h in range(HH):
                        last = mm(bank[:, c % 2, h * DV:(h + 1) * DV], F.kendT[cc * CH:(cc + 1) * CH, t, h, :],
                                  F.tok[cc * CH:(cc + 1) * CH, t, I0 + h * DV:I0 + (h + 1) * DV], start=True, stop=True)
                    last.then_inc(F.kv_done, 1)

                def tile_out(t):
                    pe.wait_ge(F.at_out, t + 1)
                    if t >= 2:
                        pe.wait_ge(F.rec_ready, t - 1)
                    pe.wait_ge(F.state_ready, 2 * t + 2)
                    for h in range(HH):
                        hv = slice(h * DV, (h + 1) * DV)
                        mm(bank[:, 2 + t % 2, hv], F.AT[:, t, h, :], F.tok[:, t, I0 + h * DV:I0 + (h + 1) * DV],
                           start=True, stop=False, skip_group_check=True)
                        for cc in range(2):
                            c = 2 * t + cc
                            last = mm(bank[cc * CH:(cc + 1) * CH, 2 + t % 2, hv], F.HQ[:, h, c * CH:(c + 1) * CH],
                                      F.ST[c][:, h, :], start=False, stop=True, skip_group_check=True)
                    last.then_inc(F.o_done, 1)

                def turn_rec(t):
                    pe.wait_ge(F.rec_ready, t + 1)
                    if t >= 2:
                        pe.wait_ge(F.rec_out, t - 1)
                    for h in range(HH):
                        last = turn(bank[:, 4 + t % 2, h * P:(h + 1) * P], F.otok[:, t, h, :], ident[:, :])
                    last.then_inc(F.rec_turned, 1)

                pe.wait_ge(F.proj_out, 2 * N_HQF + N_TOK * nt)
                chunk_kv(0)
                for t in range(nt):
                    chunk_kv(2 * t + 1)
                    tile_out(t)
                    chunk_kv(2 * t + 2)
                    if t >= 1:
                        turn_rec(t - 1)

                def gates(m):
                    k = I_MIX + 3 * (m // 2) + m % 2
                    item_in(pe, F, k)
                    w = item(F, k).rearrange("p (c n) -> p c n", n=P)
                    if m >= 2:
                        pe.wait_ge(F.mix_out, m - 1)
                    b = 4 * (m % 2)
                    for g in range(2):
                        for c in range(KC):
                            last = mm(bank[:, b + g, 0:n], w[:, g * KC + c, :], F.act_in[:, c, :],
                                      start=c == 0, stop=c == KC - 1)
                    last.then_inc(F.gate_done, 1)

                def branches(m):
                    k = I_MIX + 3 * (m // 2) + 2
                    item_in(pe, F, k)
                    w = item(F, k).rearrange("p (m c n) -> p m c n", m=2, n=P)
                    b = 4 * (m % 2)
                    for j in range(PAIRS):
                        mm(bank[:, b + 2, 0:n], w[:, m % 2, j, :], F.attnT[:, j, :], start=j == 0, stop=j == PAIRS - 1)
                    for h in range(HH):
                        last = mm(bank[:, b + 3, 0:n], w[:, m % 2, PAIRS + h, :], F.recT[:, h, :],
                                  start=h == 0, stop=h == HH - 1)
                    last.then_inc(F.mix_done, 1)

                pe.wait_ge(F.state_ready, states + 1)
                gates(0)
                turn_rec(nt - 1)
                pe.wait_ge(F.rec_out, nt)
                for m in range(0, KC, 2):
                    if m:
                        gates(m)
                    gates(m + 1)
                    branches(m)
                    branches(m + 1)

                pe.wait_ge(F.mix_out, KC)
                for k in range(N_OUT):
                    item_in(pe, F, I_OUT + k)
                    w = item(F, I_OUT + k).rearrange("p (c n) -> p c n", c=KC)
                    for t in range(nt):
                        u = k * nt + t
                        if u >= 4:
                            pe.wait_ge(F.y_out, u - 3)
                        for c in range(KC):
                            last = mm(bank[:, u % 4, 0:TW], F.mixT[:, c, t * P:(t + 1) * P], w[:, c, :],
                                      start=c == 0, stop=c == KC - 1)
                        last.then_inc(F.y_done, 1)

                for t in range(nt):
                    pe.wait_ge(F.x1_ready, t + 1)
                    for half in range(2):
                        u = 2 * t + half
                        if u >= 4:
                            pe.wait_ge(F.x1_out, u - 3)
                        for k in range(4):
                            c = 4 * half + k
                            last = turn(bank[:, 4 + u % 4, k * P:(k + 1) * P], F.x1[:, t, c * P:(c + 1) * P], ident[:, :])
                        last.then_inc(F.x1_turned, 1)

                pe.wait_ge(F.x1_out, 2 * nt)
                pe.wait_ge(F.y_out, N_OUT * nt)

                def key_scores(h):
                    pe.wait_ge(F.pq_out, 2 * h + 2)
                    for t in range(nt):
                        u = h * nt + t
                        if u >= 4:
                            pe.wait_ge(F.ks_out, u - 3)
                        for half in range(2):
                            last = mm(bank[:, 4 + u % 4, half * NK:(half + 1) * NK],
                                      F.qTp[:, 2 * h + half, t * P:(t + 1) * P], keys[:, half, :], start=True, stop=True)
                        last.then_inc(F.ks_done, 1)

                for h in range(PH):
                    item_in(pe, F, I_WQ + h)
                    w = item(F, I_WQ + h).rearrange("p (c n) -> p c n", c=KC)
                    for half in range(2):
                        b = 2 * h + half
                        if b >= 4:
                            pe.wait_ge(F.pq_out, b - 3)
                        for c in range(KC):
                            last = mm(bank[:, b % 4, 0:n], w[:, c, half * P:(half + 1) * P], F.act_in[:, c, :],
                                      start=c == 0, stop=c == KC - 1)
                        last.then_inc(F.pq_done, 1)
                    if h:
                        key_scores(h - 1)
                key_scores(PH - 1)

            front(A)
            front(B, A)

            pe.wait_ge(alpha_ready, 1)
            pe.wait_ge(B.ks_out, PH * B.nt)
            pe.wait_ge(B.pq_out, 2 * PH)

            def residual(t):
                pe.wait_ge(acc_out, t + 1)
                for n in range(2):
                    mm(bank[:, n, :], alphaI[:, :], x1.rearrange("p t d -> p (t d)")[:, bass.ds(t * D + n * 512, 512)],
                       start=True, stop=False, skip_group_check=True)

            def v_round(t, i, shared):
                mine = [s for s in range(SLOTS) if not (shared and s % GRP == GRP - 1)]
                for s in mine:
                    if s % GRP == 0:
                        pe.wait_ge(diag_ready, GPP * t + GPR * (i - EARLY_V) + s // GRP + 1)
                    pe.wait_ge(landed[s], 16 * (2 * ROUNDS * t + ROUNDS + i + 1))
                    mm(bank[:, 0, :], diag[:, s, :], rows[:, s, 0:512], start=False, stop=False, skip_group_check=True)
                    last = mm(bank[:, 1, :], diag[:, s, :], rows[:, s, 512:D], start=False, stop=False,
                              skip_group_check=True)
                    if s % GRP == GRP - 1 - shared:
                        last.then_inc(v_used, 1)

            residual(0)
            pe.wait_ge(v_used, GPR + GPR * EARLY_V)
            for i in range(EARLY_V, ROUNDS):
                v_round(0, i, False)
            with pe.Fori(1, T) as t:
                residual(t)
                with pe.Fori(0, SHARE_FROM) as i:
                    v_round(t, i, False)
                with pe.Fori(SHARE_FROM, ROUNDS) as i:
                    v_round(t, i, True)

        @block.scalar
        def _(act):
            fn = nc.scalar.activation

            def front(F):
                n, nt = F.n, F.nt
                for b in range(2 * N_HQF):
                    act.wait_ge(F.proj_done, b + 1)
                    dst, f = (F.HF, ACT.Sigmoid) if b < 4 else (F.HQ, ACT.Silu)
                    fn(dst[:, b % 4, :], bank[:, b % 4, 0:n], f).then_inc(F.proj_out, 1)

                def copy_tok(k):
                    for t in range(nt):
                        b = 2 * N_HQF + k * nt + t
                        act.wait_ge(F.proj_done, b + 1)
                        fn(F.tok[:, t, k * TW:(k + 1) * TW], bank[:, b % 4, 0:TW],
                           ACT.Copy if k * TW < G0 else ACT.Silu).then_inc(F.proj_out, 1)

                if F is A:
                    act.wait_ge(lb_arg, 1)
                    fn(lbl[:, :, :], lbl[:, :, :], ACT.Exp).then_inc(lb_exp, 1)
                    act.wait_ge(trig_arg, 1)
                    fn(trig[:, :, :, :], trig[:, :, :, :], ACT.Sin).then_inc(trig_ready, 1)
                for k in range(TOK_EARLY):
                    copy_tok(k)

                for h in range(HH):
                    act.wait_ge(F.fg_ready, h + 1)
                    fn(F.HF[:, h, :], F.HF[:, h, :], ACT.Ln).then_inc(F.hgrn_ln, 1)
                for h in range(HH):
                    act.wait_ge(F.bcum_ready, h + 1)
                    fn(F.SQ[:, h % 2, :], F.BC[:, h % 2, :], ACT.Exp).then_inc(F.hgrn_exp, 1)
                    fn(F.HF[:, h, :], F.HF[:, h, :], ACT.Exp).then_inc(F.hgrn_exp, 1)
                    act.wait_ge(F.hgrn_exp, 3 * h + 2)
                    fn(F.BC[:, h % 2, :], F.BC[:, h % 2, :], ACT.Exp, scale=-1.0).then_inc(F.hgrn_exp, 1)

                for t in range(nt):
                    for part in range(3):
                        u = 3 * t + part
                        act.wait_ge(F.qk_turned, u + 1)
                        src = bank[0:HD, 4 + u % 4, :]
                        if part < 2:
                            src = src.rearrange("p (h c q) -> p h c q", h=4, c=2)
                            dst = F.qT[:, 2 * t:2 * t + 2, 4 * part:4 * part + 4, :].rearrange("p c h q -> p h c q")
                        else:
                            src = src[:, 0:KVH * P].rearrange("p (h q) -> p h q", h=KVH)
                            dst = F.kT[:, t, :, :]
                        fn(dst, src, ACT.Copy).then_inc(F.qk_out, 1)
                for c in range(F.nc):
                    act.wait_ge(F.score_done, c + 1)
                    w = CH if c == 0 and F is A else P
                    fn(F.SC[:, c, :, 0:w], bank[:, 4 + c % 4, :].rearrange("p (j k) -> p j k", j=PAIRS)[:, :, 0:w],
                       ACT.Copy, scale=SCALE).then_inc(F.score_out, 1)
                for k in range(TOK_EARLY, N_TOK):
                    copy_tok(k)
                act.wait_ge(F.soft_arg, 1)
                fn(F.SC, F.SC, ACT.Exp).then_inc(F.soft_exp, 1)
                fn(F.snk, F.snk, ACT.Exp).then_inc(F.soft_exp, 1)

                def copy_wT(c):
                    act.wait_ge(F.w_turned, c + 1)
                    fn(F.PT[:, c, :, :], bank[:, 4 + c % 2, :].rearrange("p (j k) -> p j k", j=PAIRS),
                       ACT.Copy).then_inc(F.w_outT, 1)

                copy_wT(0)
                for c in range(F.nc):
                    if c + 1 < F.nc:
                        copy_wT(c + 1)
                    act.wait_ge(F.av_done, c + 1)
                    fn(F.attnT[:, :, c * CH:(c + 1) * CH],
                       bank[:, 6 + c % 2, 0:PAIRS * CH].rearrange("p (j q) -> p j q", j=PAIRS), ACT.Copy).then_inc(F.av_out, 1)
                for t in range(nt):
                    act.wait_ge(F.kend_turned, t + 1)
                    fn(F.kendT[:, t, :, :], bank[:, 4 + t % 2, :].rearrange("p (h k) -> p h k", h=HH),
                       ACT.Copy).then_inc(F.kend_out, 1)

                def copy_rec(t):
                    act.wait_ge(F.rec_turned, t + 1)
                    fn(F.recT[:, :, t * P:(t + 1) * P], bank[:, 4 + t % 2, :].rearrange("p (h k) -> p h k", h=HH),
                       ACT.Copy).then_inc(F.rec_out, 1)

                for t in range(nt):
                    act.wait_ge(F.ms_ready, t + 1)
                    fn(F.rms[:, t, :], F.rms[:, t, :], ACT.Sqrt).then_inc(F.rms_root, 1)
                    if t:
                        copy_rec(t - 1)
                copy_rec(nt - 1)
                if F is B:
                    act.wait_ge(gexp_arg, 1)
                    fn(gexp, gexp, ACT.Exp).then_inc(gexp_done, 1)
                for m in range(KC):
                    act.wait_ge(F.gate_done, m + 1)
                    if m >= 2:
                        act.wait_ge(F.mix_out, m - 1)
                    for k in range(2):
                        fn(F.sig[:, m % 2, k, :], bank[:, 4 * (m % 2) + k, 0:n], ACT.Sigmoid).then_inc(F.gate_ready, 1)

                if F is B:
                    act.wait_ge(hid_ready, 1)
                    fn(hid, hid, ACT.Gelu).then_inc(gelu_done, 1)

                def copy_x1(u):
                    act.wait_ge(F.x1_turned, u + 1)
                    fn(F.act_in[:, u % 2 * 4:u % 2 * 4 + 4, u // 2 * P:(u // 2 + 1) * P],
                       bank[:, 4 + u % 4, :].rearrange("p (c k) -> p c k", c=4), ACT.Copy).then_inc(F.x1_out, 1)

                for t in range(nt):
                    act.wait_ge(F.var_ready, t + 1)
                    fn(rstd[:, :], rstd[:, :], ACT.Sqrt).then_inc(F.std_ready, 1)
                    if t:
                        copy_x1(2 * t - 2)
                        copy_x1(2 * t - 1)
                copy_x1(2 * nt - 2)
                copy_x1(2 * nt - 1)

                def copy_scores(h):
                    for t in range(nt):
                        u = h * nt + t
                        act.wait_ge(F.ks_done, u + 1)
                        fn(F.s12[:, t, h * 2 * NK:(h + 1) * 2 * NK], bank[:, 4 + u % 4, 0:2 * NK], ACT.Copy).then_inc(F.ks_out, 1)

                for h in range(PH):
                    for b in (2 * h, 2 * h + 1):
                        act.wait_ge(F.pq_done, b + 1)
                        fn(F.qTp[:, b, :], bank[:, b % 4, 0:n], ACT.Copy).then_inc(F.pq_out, 1)
                    if h:
                        copy_scores(h - 1)
                copy_scores(PH - 1)

            front(A)
            front(B)

            def diagonals(t, i, shared):
                for g in range(GPR):
                    act.wait_ge(v_used, GPP * t + GPR * i + g + 1)
                    act.sem_inc(act_gate, 1)
                    for k in range(GRP - shared):
                        s = g * GRP + k
                        last = fn(diag[:, s, :], ident[:, :], ACT.Copy, scale=wv[:, bass.ds(i * SLOTS + s, 1)])
                    last.then_inc(diag_ready, 1)

            act.wait_ge(wv_ready, 1)
            for i in range(EARLY_V, ROUNDS):
                diagonals(0, i, False)
            act.wait_ge(var2_ready, 1)
            fn(rstd[:, :], rstd[:, :], ACT.Sqrt).then_inc(std2_ready, 1)
            with act.Fori(1, T) as t:
                act.wait_ge(gexp_arg, t + 1)
                fn(gexp, gexp, ACT.Exp).then_inc(gexp_done, 1)
                act.wait_ge(hid_ready, t + 1)
                fn(hid, hid, ACT.Gelu).then_inc(gelu_done, 1)
                act.wait_ge(wv_ready, t + 1)
                act.sem_inc(act_gate, 1)
                with act.Fori(0, SHARE_FROM) as i:
                    diagonals(t, i, False)
                with act.Fori(SHARE_FROM, ROUNDS) as i:
                    diagonals(t, i, True)
                act.wait_ge(var2_ready, t + 1)
                fn(rstd[:, :], rstd[:, :], ACT.Sqrt).then_inc(std2_ready, 1)

        @block.vector
        def _(dve):
            v = nc.vector
            ch = Chain(dve)

            def steps(*ins):
                for x in ins:
                    ch(x())
                ch.wait()

            dve.wait_ge(consts_in, 16 * CONSTS)
            steps(lambda: v.tensor_tensor(lbm[:, :], lbl[:, 0, :], lbl[:, 1, :], ALU.max),
                  lambda: v.tensor_copy(pos_f[:, :], pos_i[:, :]),
                  lambda: v.tensor_scalar(alphaI[:, :], ident[:, :], ALPHA, None, ALU.mult),
                  lambda: v.memset(v_last[0:CH, :], 0.0))
            dve.sem_inc(alpha_ready, 1)
            v.tensor_tensor(lbl[:, :, :], lbl[:, :, :], lbm[:, :].unsqueeze(1).to_broadcast([P, 2, HH]), ALU.subtract).then_inc(lb_arg, 1)
            steps(lambda: v.tensor_tensor(ang[:, :, :], pos_f[:, :].unsqueeze(2).to_broadcast([P, T, HALF]),
                                          freq[:, :].unsqueeze(1).to_broadcast([P, T, HALF]), ALU.mult))
            steps(lambda: v.tensor_scalar(turns[:, :, :], ang[:, :, :], 1.0 / (2 * math.pi), None, ALU.mult))
            steps(lambda: v.tensor_scalar(turns[:, :, :], turns[:, :, :], MAGIC, None, ALU.add))
            steps(lambda: v.tensor_scalar(turns[:, :, :], turns[:, :, :], MAGIC, None, ALU.subtract))
            for part in (PI2_A, PI2_B, PI2_C):
                steps(lambda: v.scalar_tensor_tensor(out=ang[:, :, :], in0=turns[:, :, :], scalar=-part,
                                                     in1=ang[:, :, :], op0=ALU.mult, op1=ALU.add))
            steps(lambda: v.tensor_scalar(trig[:, 1, :, :], ang[:, :, :], 3.1415925, -3.1415925, ALU.min, ALU.max))
            steps(lambda: v.tensor_scalar(trig[:, 0, :, :], trig[:, 1, :, :], -1.0, None, ALU.mult))
            steps(lambda: v.tensor_tensor(trig[:, 0, :, :], trig[:, 0, :, :], trig[:, 1, :, :], ALU.min))
            steps(lambda: v.tensor_scalar(trig[:, 0, :, :], trig[:, 0, :, :], math.pi / 2, None, ALU.add))
            dve.sem_inc(trig_arg, 1)
            dve.wait_ge(lb_exp, 1)
            steps(lambda: v.tensor_tensor(lbm[:, :], lbl[:, 0, :], lbl[:, 1, :], ALU.add))
            steps(lambda: v.reciprocal(lbm[:, :], lbm[:, :]))
            steps(lambda: v.tensor_tensor(lbv[:, :], lbl[:, 0, :], lbm[:, :], ALU.mult))
            steps(lambda: v.tensor_scalar(omlb[:, :], lbv[:, :], -1.0, 1.0, ALU.mult, ALU.add))

            def rows_until(q):
                while done[0] < q:
                    k = done[0]
                    s = k % SLOTS
                    if k < NE:
                        dve.wait_ge(landed[s], 16 * (k // SLOTS + 1))
                        last = v.tensor_tensor_reduce(rows[:, s, :], rows[:, s, :], x1[:, 0, :], 1.0, 0.0,
                                                      ALU.mult, ALU.add, hid[:, k:k + 1])
                        if s % GRP == GRP - 1:
                            last.then_inc(u_used, 1)
                    else:
                        if k == NE:
                            dve.wait_ge(u_used, GPP)
                            dve.sem_inc(hid_ready, 1)
                            weights(0)
                            dve.sem_inc(v_shared, GPP)
                            steps(lambda: v.memset(acc, 0.0))
                        j = k - NE
                        dve.wait_ge(landed[s], 16 * (k // SLOTS + 1))
                        ch.wait()
                        ch(v.scalar_tensor_tensor(out=acc, in0=rows[:, s, :], scalar=wv[:, j:j + 1], in1=acc,
                                                  op0=ALU.mult, op1=ALU.add))
                        if s % GRP == GRP - 1:
                            ch.wait()
                            dve.sem_inc(v_used, 1)
                    done[0] += 1

            done = [0]

            def front(F, rows_until):
                n, nt, nch = F.n, F.nt, F.nc
                rows_until(AT_FG)
                dve.wait_ge(F.proj_out, 4)
                for h in range(HH):
                    ch(v.tensor_scalar(F.HF[:, h, :], F.HF[:, h, :], omlb[:, h:h + 1], lbv[:, h:h + 1], ALU.mult, ALU.add))
                ch.wait()
                for h in range(HH):
                    v.tensor_scalar(F.KH[:, h, :], F.HF[:, h, :], -1.0, 1.0, ALU.mult, ALU.add).then_inc(F.fg_ready, 1)

                rows_until(AT_ROPE)
                dve.wait_ge(trig_ready, 1)
                dve.wait_ge(F.proj_out, 2 * N_HQF + 3 * nt)
                heads = F.tok[:, :, 0:V0].rearrange("p t (h d) -> p t h d", d=HD)
                first, second = heads[:, :, :, 0:HALF], heads[:, :, :, HALF:ROT]
                full = [P, nt, HEADS + KVH, HALF]
                cos = trig[:, 0, F.t0:F.t0 + nt, :].unsqueeze(2).to_broadcast(full)
                sin = trig[:, 1, F.t0:F.t0 + nt, :].unsqueeze(2).to_broadcast(full)
                for k in range(4):
                    ch(v.tensor_tensor(F.rot[:, k, :, :, :], (first, second, second, first)[k],
                                       (cos, sin, cos, sin)[k], ALU.mult))
                ch.wait()
                ch(v.tensor_tensor(first, F.rot[:, 0, :, :, :], F.rot[:, 1, :, :, :], ALU.subtract))
                v.tensor_tensor(second, F.rot[:, 2, :, :, :], F.rot[:, 3, :, :, :], ALU.add).then_inc(F.rope_done, 1)

                rows_until(AT_HGRN)

                def cumulate(h):
                    dve.wait_ge(F.hgrn_ln, h + 1)
                    steps(lambda: v.tensor_tensor_scan(F.BC[:, h % 2, :], chunk_mask[:, 0:n], F.HF[:, h, :], 0.0,
                                                       ALU.mult, ALU.add))
                    bc, hf = (z.rearrange("p (c l) -> p c l", l=CH) for z in (F.BC[:, h % 2, :], F.HF[:, h, :]))
                    v.tensor_tensor(hf, bc[:, :, CH - 1:CH].to_broadcast([P, nch, CH]), bc,
                                    ALU.subtract).then_inc(F.bcum_ready, 1)

                def decayed(h):
                    dve.wait_ge(F.hgrn_exp, 3 * h + 1)
                    ch(v.tensor_tensor(F.HQ[:, h, :], F.HQ[:, h, :], F.SQ[:, h % 2, :], ALU.mult))
                    ch(v.tensor_copy(F.decay[:, h, :], F.SQ[:, h % 2, :].rearrange("p (c l) -> p c l", l=CH)[:, :, CH - 1]))
                    dve.wait_ge(F.hgrn_exp, 3 * h + 2)
                    ch(v.tensor_tensor(F.HF[:, h, :], F.HF[:, h, :], F.KH[:, h, :], ALU.mult))
                    ch.wait()
                    dve.wait_ge(F.hgrn_exp, 3 * h + 3)
                    steps(lambda: v.tensor_tensor(F.KH[:, h, :], F.KH[:, h, :], F.BC[:, h % 2, :], ALU.mult))

                dve.wait_ge(F.proj_out, 2 * N_HQF)
                cumulate(0)
                cumulate(1)
                decayed(0)
                cumulate(2)
                decayed(1)
                cumulate(3)
                decayed(2)
                decayed(3)
                dve.sem_inc(F.kq_ready, 1)

                rows_until(AT_SOFT)
                if F is A:
                    steps(lambda: v.memset(F.SC[:, 0, :, CH:P], NEG))
                dve.wait_ge(F.score_out, nch)
                steps(lambda: v.tensor_reduce(F.mx, F.SC, AX_X, ALU.max),
                      lambda: v.memset(F.v_even[CH:P, :, :], 0.0),
                      lambda: v.memset(F.v_odd[0:CH, :, :], 0.0),
                      lambda: v.tensor_copy(F.v_even[0:CH, :, :], F.tok[0:CH, :, V0:I0]),
                      lambda: v.tensor_copy(F.v_odd[CH:P, :, :], F.tok[CH:P, :, V0:I0]))
                if F is A:
                    steps(lambda: v.tensor_copy(v_last[CH:P, :], F.tok[CH:P, 0, V0:I0]),
                          lambda: v.tensor_copy(k_last[:, :, :], F.kT[:, 0, :, CH:P]))
                dve.sem_inc(F.vz_ready, 1)
                sink = sinkc[:, :].unsqueeze(1).to_broadcast([P, nch, PAIRS])
                steps(lambda: v.tensor_tensor(F.mx, F.mx, sink, ALU.max))
                wide = [P, nch, PAIRS, P]
                steps(lambda: v.tensor_tensor(F.SC, F.SC, F.mx.unsqueeze(3).to_broadcast(wide), ALU.subtract),
                      lambda: v.tensor_tensor(F.snk, sink, F.mx, ALU.subtract))
                dve.sem_inc(F.soft_arg, 1)
                dve.wait_ge(F.proj_out, 2 * N_HQF + N_TOK * nt)
                gate = F.tok[:, :, G0:G0 + HH * DV].rearrange("p t (h e) -> p t h e", h=HH)
                steps(lambda: v.tensor_tensor(gate, gate, normg[:, :].unsqueeze(1).unsqueeze(1).to_broadcast([P, nt, HH, DV]),
                                              ALU.mult))
                rows_until(AT_SOFT2)
                dve.wait_ge(F.soft_exp, 2)
                steps(lambda: v.tensor_reduce(F.den, F.SC, AX_X, ALU.add))
                steps(lambda: v.tensor_tensor(F.den, F.den, F.snk, ALU.add))
                steps(lambda: v.reciprocal(F.den, F.den))
                v.tensor_tensor(F.SC, F.SC, F.den.unsqueeze(3).to_broadcast(wide), ALU.mult).then_inc(F.soft_done, 1)

                rows_until(AT_CAUSAL)
                dve.wait_ge(F.w_outT, nch)
                dve.wait_ge(F.av_done, nch)
                steps(lambda: v.memset(F.AT, 0.0))
                if F is A:
                    steps(lambda: v.memset(F.ST[0], 0.0))
                for t in range(nt):
                    dve.wait_ge(F.at_done, t + 1)
                    v.copy_predicated(F.AT[:, t, :, :], causal[:, :].unsqueeze(1).to_broadcast([P, HH, P]),
                                      bank[:, 6 + t % 2, :].rearrange("p (h l) -> p h l", h=HH)).then_inc(F.at_out, 1)

                def state(c):
                    dve.wait_ge(F.kv_done, c + 1)
                    dve.wait_ge(F.state_ready, c + 1)
                    for h in range(HH):
                        last = v.scalar_tensor_tensor(out=F.ST[c + 1][:, h, :], in0=F.ST[c][:, h, :],
                                                      scalar=F.decay[:, h, c:c + 1],
                                                      in1=bank[:, c % 2, h * DV:(h + 1) * DV], op0=ALU.mult, op1=ALU.add)
                    last.then_inc(F.state_ready, 1)

                def norm_rec(t):
                    dve.wait_ge(F.o_done, t + 1)
                    o = bank[:, 2 + t % 2, :].rearrange("p (h e) -> p h e", h=HH)
                    steps(lambda: v.tensor_copy(F.otok[:, t, :, :], o))
                    steps(lambda: v.tensor_tensor(F.osq, F.otok[:, t, :, :], F.otok[:, t, :, :], ALU.mult))
                    steps(lambda: v.tensor_reduce(F.rms[:, t, :], F.osq, AX_X, ALU.add))
                    v.tensor_scalar(F.rms[:, t, :], F.rms[:, t, :], 1.0 / DV, RMS_EPS, ALU.mult, ALU.add).then_inc(F.ms_ready, 1)
                    dve.wait_ge(F.rms_root, t + 1)
                    steps(lambda: v.reciprocal(F.rms[:, t, :], F.rms[:, t, :]))
                    steps(lambda: v.tensor_tensor(F.otok[:, t, :, :], F.otok[:, t, :, :],
                                                  F.rms[:, t, :].unsqueeze(2).to_broadcast([P, HH, DV]), ALU.mult))
                    v.tensor_tensor(F.otok[:, t, :, :], F.otok[:, t, :, :],
                                    F.tok[:, t, G0:G0 + HH * DV].rearrange("p (h e) -> p h e", h=HH),
                                    ALU.mult).then_inc(F.rec_ready, 1)

                states = nch if F is A else nch - 1
                dve.sem_inc(F.state_ready, 1)
                state(0)
                for t in range(nt):
                    for c in (2 * t + 1, 2 * t + 2):
                        if c < states:
                            state(c)
                    norm_rec(t)
                    rows_until(AT_REC + 4 * t)

                for m in range(KC):
                    rows_until(AT_MIX + MIX_STEP * m)
                    b = 4 * (m % 2)
                    dve.wait_ge(F.gate_ready, 2 * m + 2)
                    dve.wait_ge(F.mix_done, m + 1)
                    for k in range(2):
                        ch(v.tensor_tensor(F.sig[:, m % 2, k, :], F.sig[:, m % 2, k, :], bank[:, b + 2 + k, 0:n], ALU.mult))
                    ch.wait()
                    v.tensor_tensor(F.mixT[:, m, :], F.sig[:, m % 2, 0, :], F.sig[:, m % 2, 1, :], ALU.add).then_inc(F.mix_out, 1)

                dve.wait_ge(F.x_in, 16)
                dve.wait_ge(ln1_in, 32)
                for k in range(N_OUT):
                    rows_until(AT_OUT + OUT_STEP * k)
                    for t in range(nt):
                        u = k * nt + t
                        dve.wait_ge(F.y_done, u + 1)
                        xs = F.x1[:, t, k * TW:(k + 1) * TW]
                        v.scalar_tensor_tensor(out=xs, in0=xs, scalar=ALPHA, in1=bank[:, u % 4, 0:TW],
                                               op0=ALU.mult, op1=ALU.add).then_inc(F.y_out, 1)
                dve.wait_ge(F.y_out, N_OUT * nt)
                for t in range(nt):
                    layer_norm(t, F.x1[:, t, :], F.x1[:, t, :], F.var_ready, F.std_ready, F.x1_ready)
                    rows_until(AT_LN + LN_STEP * t)

            def layer_norm(t, src, dst, var_ready, std_ready, ready):
                for n in range(2):
                    ch(v.bn_stats(stats[:, n, :], src[:, n * 512:(n + 1) * 512]))
                ch.gate()
                steps(lambda: v.bn_aggr(mv[:, :], stats[:, :, :]))
                v.tensor_scalar(rstd[:, :], mv[:, 1:2], LN_EPS, None, ALU.add).then_inc(var_ready, 1)
                dve.wait_ge(std_ready, t + 1)
                steps(lambda: v.reciprocal(rstd[:, :], rstd[:, :]))
                steps(lambda: v.tensor_scalar(dst, src, mv[:, 0:1], rstd[:, 0:1], ALU.subtract, ALU.mult))
                steps(lambda: v.tensor_tensor(dst, dst, ln_gb[:, 0, :], ALU.mult))
                v.tensor_tensor(dst, dst, ln_gb[:, 1, :], ALU.add).then_inc(ready, 1)
                dve.wait_ge(ready, t + 1)

            eidx_all = eidx.rearrange("p t e -> p (t e)")
            s12_all = B.s12.rearrange("p t s -> p (t s)")
            x1_all = x1.rearrange("p t d -> p (t d)")

            def top16(values, best, index, n):
                for half in range(2):
                    part = slice(8 * half, 8 * half + 8)
                    for b in range(n):
                        ch(v.max(best(b)[:, part], values(b)))
                    ch.gate()
                    for b in range(n):
                        ch(v.max_index(index(b)[:, part], best(b)[:, part], values(b)))
                    ch.gate()
                    if half == 0:
                        for b in range(n):
                            ch(v.match_replace(values(b), best(b)[:, part], values(b), LOWEST))
                        ch.gate()

            def route(hs, values, cand, onehot, picked, store):
                nh = len(hs)
                h0 = hs[0]
                sums, flat = [P, nh, TOPK, TOPK], [P, nh * TOPK, TOPK]
                top16(values, lambda b: top[:, h0 + b // 2, b % 2, :], lambda b: topi[:, h0 + b // 2, b % 2, :], 2 * nh)
                tp, tf = top[:, h0:h0 + nh, :, :], topf[:, h0:h0 + nh, :, :]
                steps(lambda: v.tensor_copy(tf, topi[:, h0:h0 + nh, :, :]),
                      lambda: v.tensor_tensor(cand, tp[:, :, 0, :].unsqueeze(3).to_broadcast(sums),
                                              tp[:, :, 1, :].unsqueeze(2).to_broadcast(sums), ALU.add))
                ch.gate()
                top16(lambda h: cand[:, h, :, :].rearrange("p i j -> p (i j)"), lambda h: sco[:, h0 + h, :],
                      lambda h: sci[:, h0 + h, :], nh)
                ei = slice(h0 * TOPK, (h0 + nh) * TOPK)
                hi, hf = half_i[:, h0:h0 + nh, :], half_f[:, h0:h0 + nh, :]
                for half, e in ((0, e1), (1, e2)):
                    op, arg = (ALU.logical_shift_right, 4) if half == 0 else (ALU.bitwise_and, 15)
                    steps(lambda: v.tensor_scalar(hi, sci[:, h0:h0 + nh, :], arg, None, op))
                    steps(lambda: v.tensor_copy(hf, hi))
                    steps(lambda: v.tensor_tensor(onehot, hf.rearrange("p h k -> p (h k)").unsqueeze(2).to_broadcast(flat),
                                                  iota16[:, :].unsqueeze(1).to_broadcast(flat), ALU.is_equal))
                    oh = onehot.rearrange("p (h k) j -> p h k j", h=nh)
                    steps(lambda: v.tensor_tensor(oh, oh, tf[:, :, half, :].unsqueeze(2).to_broadcast(sums), ALU.mult))
                    steps(lambda: v.tensor_reduce(e[:, ei], onehot, AX_X, ALU.add))
                steps(lambda: v.scalar_tensor_tensor(out=e1[:, ei], in0=e1[:, ei], scalar=float(NK), in1=e2[:, ei],
                                                     op0=ALU.mult, op1=ALU.add))
                store(ei)

            def softmax_arg():
                v.tensor_tensor(gexp, sco, sco[:, :, 0:1].to_broadcast([P, PH, TOPK]), ALU.subtract).then_inc(gexp_arg, 1)

            def route_tile(t):
                ch.gate()
                ch(v.tensor_copy(scur.rearrange("p b k -> p (b k)"),
                                 s12_all[:, bass.ds((t - 1) * (2 * PH * NK), 2 * PH * NK)]))
                ch.gate()

                def store(ei):
                    ch.gate()
                    v.tensor_copy(eidx_all[:, bass.ds(t * NE, NE)], e1).then_inc(idx_ready, PH)

                route(range(PH), lambda b: scur[:, b, :], cand, onehot, picked, store)
                softmax_arg()

            def hidden(t):
                ch.gate()
                ch(v.tensor_copy(x1cur, x1_all[:, bass.ds(t * D, D)]))
                start = ch.n
                with dve.Fori(0, ROUNDS) as i:
                    ch.enter(i, 1)
                    for s in range(SLOTS):
                        if s == 0:
                            ch.wait()
                        dve.wait_ge(landed[s], 16 * (2 * ROUNDS * t + i + 1))
                        last = v.tensor_tensor_reduce(rows[:, s, :], rows[:, s, :], x1cur, 1.0, 0.0,
                                                      ALU.mult, ALU.add, hid_r[:, s:s + 1])
                        if s % GRP == GRP - 1:
                            last.then_inc(u_used, 1)
                    dve.wait_ge(u_used, GPP * t + GPR * i + GPR)
                    dve.sem_inc(route_gate, 1)
                    ch(v.tensor_copy(hid[:, bass.ds(i * SLOTS, SLOTS)], hid_r))
                    ch.leave(start, ROUNDS)
                ch.wait()
                dve.sem_inc(hid_ready, 1)

            def weights(t):
                dve.wait_ge(gexp_done, t + 1)
                steps(lambda: v.tensor_reduce(gsum, gexp, AX_X, ALU.add))
                steps(lambda: v.reciprocal(gsum, gsum))
                steps(lambda: v.tensor_tensor(gexp, gexp, gsum.unsqueeze(2).to_broadcast([P, PH, TOPK]), ALU.mult))
                dve.wait_ge(gelu_done, t + 1)
                v.tensor_tensor(wv, hid, gexp.rearrange("p h k -> p (h k)"), ALU.mult).then_inc(wv_ready, 1)
                dve.wait_ge(wv_ready, t + 1)

            def share(t):
                start = ch.n
                with dve.Fori(SHARE_FROM, ROUNDS) as i:
                    ch.enter(i - SHARE_FROM, GPR)
                    for s in range(GRP - 1, SLOTS, GRP):
                        dve.wait_ge(landed[s], 16 * (2 * ROUNDS * t + ROUNDS + i + 1))
                        dve.sem_inc(route_gate, 1)
                        ch.wait()
                        ch(v.scalar_tensor_tensor(out=acc, in0=rows[:, s, :], scalar=wv[:, bass.ds(i * SLOTS + s, 1)],
                                                  in1=acc, op0=ALU.mult, op1=ALU.add))
                        ch.wait()
                        dve.sem_inc(v_shared, 1)
                    ch.leave(start, ROUNDS - SHARE_FROM)

            def start_share():
                dve.sem_inc(v_shared, GPR * SHARE_FROM)
                ch(v.memset(acc, 0.0))

            def second_norm(t, count):
                dve.wait_ge(v_used, count)
                dve.wait_ge(y_free, t + 1)
                dve.sem_inc(route_gate, 1)
                steps(lambda: v.tensor_tensor(acc, acc, psum_acc, ALU.add))
                dve.sem_inc(acc_out, 1)
                layer_norm(t, acc, ybuf, var2_ready, std2_ready, y2_ready)

            psum_acc = bank[:, 0:2, :].rearrange("p b n -> p (b n)")
            front(A, lambda q: None)
            for h in range(PH):
                dve.wait_ge(A.ks_out, h + 1)
                dve.sem_inc(route_gate, 1)

                def store(ei):
                    v.tensor_copy(eidx[:, 0, ei], e1[:, ei]).then_inc(idx_ready, 1)

                route(range(h, h + 1), lambda b: A.s12[:, 0, (2 * h + b) * NK:(2 * h + b + 1) * NK],
                      cand0.unsqueeze(1), onehot0, picked0, store)
                rows_until(ROUTE_ROWS * (h - 1))
            softmax_arg()
            front(B, rows_until)
            rows_until(NE + EARLY_V * SLOTS)
            dve.wait_ge(B.ks_out, PH * B.nt)
            route_tile(1)
            dve.wait_ge(ln2_in, 32)
            second_norm(0, GPP + GPR)
            start = ch.n
            with dve.Fori(1, T - 1) as t:
                ch.enter(t - 1, PER_TILE)
                hidden(t)
                weights(t)
                start_share()
                route_tile(t + 1)
                share(t)
                second_norm(t, GPP * (t + 1) + GPR)
                ch.leave(start, T - 2)
            hidden(T - 1)
            weights(T - 1)
            start_share()
            share(T - 1)
            second_norm(T - 1, GPP * T + GPR)

        @block.gpsimd
        def _(pool):
            pool.sem_inc(v_used, GPR)
            pool.sem_inc(v_shared, GPR)
            pool.sem_inc(acc_out, 1)
            eidx_all = eidx.rearrange("p t e -> p (t e)")

            def gather(t, table, phase, i, g, free, count):
                if phase == 0 and g == 0:
                    pool.wait_ge(idx_ready, PH * t + i + 1)
                if free is v_used:
                    pool.wait_ge(v_shared, count)
                    pool.sem_inc(pool_gate, 1)
                pool.wait_ge(free, count)
                pool.sem_inc(pool_gate, 1)
                sl = slice(g * GRP, (g + 1) * GRP)
                nc.gpsimd.tensor_copy(cur[:, sl], eidx_all[:, bass.ds(t * NE + i * SLOTS + g * GRP, GRP)]).then_inc(cur_ready, 1)
                pool.wait_ge(cur_ready, 2 * GPP * t + GPP * phase + GPR * i + g + 1)
                pool.sem_inc(pool_gate, 1)
                for s in range(g * GRP, (g + 1) * GRP):
                    pool.indirect_dma_start(rows[:, s, :], None, table,
                                            bass.IndirectOffsetOnAxis(cur[:, s:s + 1], 0)).then_inc(landed[s], 16)

            with pool.Fori(0, T) as t:
                for phase, table, used, credit in ((0, u_rows, u_used, 0), (1, v_rows, v_used, GPR)):
                    for g in range(GPR):
                        if phase == 0:
                            gather(t, table, phase, 0, g, v_used, GPP * t + g + 1)
                        else:
                            gather(t, table, phase, 0, g, u_used, GPP * t + GPP - GPR + g + 1)
                    with pool.Fori(1, ROUNDS) as i:
                        for g in range(GPR):
                            gather(t, table, phase, i, g, used, credit + GPP * t + GPR * (i - 1) + g + 1)


def kernel(**inputs):
    import numpy as np
    import concourse.bacc as bacc
    from concourse.bass_utils import run_bass_kernel_spmd

    nc = bacc.Bacc("TRN2", target_bir_lowering=False, num_devices=1)
    arrays = {}

    def dram(name, a):
        a = np.ascontiguousarray(a)
        arrays[name] = a
        return nc.dram_tensor(name, a.shape, mybir.dt.from_np(a.dtype), kind="ExternalInput").ap()

    def get(name):
        return np.asarray(inputs[name])

    def blocks(w, n):
        return w.reshape(w.shape[0] // P, P, n, w.shape[1] // n).transpose(2, 1, 0, 3).reshape(n, P, -1)

    x = get("x")[0]
    w_in = get("w_in")[0]
    widths = (HEADS * HD, KVH * HD, KVH * HD, HH * DK, HH * DK, HH * DV, HH * DV, D, D)
    q, k, v, hq, hf, hi, hg, ga, gh = np.split(w_in, np.cumsum(widths)[:-1], axis=1)
    gates = [blocks(w, KC) for w in (ga, gh)]
    branch = [blocks(get(n)[0], KC) for n in ("w_proj_attn", "w_proj_hgrn")]
    mix = []
    for m in range(0, KC, 2):
        mix += [np.concatenate([g[k] for g in gates], axis=1) for k in (m, m + 1)]
        mix.append(np.concatenate([w[k] for k in (m, m + 1) for w in branch], axis=1))
    items = np.concatenate([blocks(np.concatenate([hf, hq], axis=1), N_HQF),
                            blocks(np.concatenate([q, k, v, hi, hg], axis=1), N_TOK), np.stack(mix),
                            blocks(get("w_out")[0], N_OUT), blocks(get("peer_wq")[0], N_WQ)])
    causal = np.kron(np.eye(2, dtype=np.uint32), np.triu(np.ones((CH, CH), np.uint32)))
    chunk = np.tile((np.arange((T - 1) * P) % CH != 0).astype(np.float32), (P, 1))
    freq = (np.float32(500000.0) ** (-np.arange(0, ROT, 2, dtype=np.float32) / np.float32(ROT))).astype(np.float32)
    args = [
        dram("x_d", x), dram("xT_d", x.T),
        dram("w_items_d", items),
        dram("keysT_d", get("peer_keys")[0].transpose(2, 0, 1)),
        dram("pos_d", get("positions")[0].reshape(T, P).T),
        dram("freq_d", freq),
        dram("sinks_d", get("attn_sinks")[0].reshape(PAIRS, 2).T),
        dram("lb_d", get("hgrn_lb").reshape(2, HH, DK).transpose(2, 0, 1)),
        dram("norm_g_d", get("hgrn_norm_g")[0]),
        dram("ln1_d", np.stack([get("ln1_g")[0], get("ln1_b")[0]])),
        dram("ln2_d", np.stack([get("ln2_g")[0], get("ln2_b")[0]])),
        dram("ident_d", np.eye(P, dtype=np.float32)), dram("causal_d", causal), dram("chunk_d", chunk),
        dram("iota_d", np.tile(np.arange(TOPK, dtype=np.float32), (P, 1))),
        dram("u_d", get("peer_u")[0]), dram("v_d", get("peer_v")[0]),
    ]
    out = nc.dram_tensor("out_d", (S, D), F32, kind="ExternalOutput").ap()
    build(nc, *args, out)
    r = run_bass_kernel_spmd(nc, [arrays], core_ids=[0])
    return r.results[0]["out_d"].reshape(1, S, D)
```

```python
import math
from contextlib import ExitStack

import concourse.bass as bass
from concourse import mybir

P = 128
F32 = mybir.dt.float32
U32 = mybir.dt.uint32
I32 = mybir.dt.int32
ALU = mybir.AluOpType
ACT = mybir.ActivationFunctionType
AX_X = mybir.AxisListType.X

S, D = 512, 1024
T = S // P
KC = D // P
CH = 64
NC = S // CH
HEADS, KVH, HD = 8, 2, 64
PAIRS = HEADS // 2
ROT = HD // 4
HALF = ROT // 2
HH, DK, DV = 4, 128, 128
TOKW = HEADS * HD + 2 * KVH * HD + 2 * HH * DV
K0 = HEADS * HD
V0 = K0 + KVH * HD
I0 = V0 + KVH * HD
G0 = I0 + HH * DV
PH, NK, TOPK = 8, 128, 16
NE = PH * TOPK
SCALE = 1.0 / math.sqrt(HD)
NEG = -1e30
LOWEST = -3.0e38
ALPHA = 2.0 ** 0.25
LN_EPS = 1e-5
RMS_EPS = 1e-6

RING, ITEMW = 3, 2048
TW = 256
N_HQF, N_TOK, N_MIX, N_OUT, N_WQ = 4, TOKW // TW, 3 * KC // 2, D // TW, PH
TOK_EARLY = 5
I_TOK = N_HQF
I_MIX = I_TOK + N_TOK
I_OUT = I_MIX + N_MIX
I_WQ = I_OUT + N_OUT
ITEMS = I_WQ + N_WQ
KEPT = N_HQF
RINGED = ITEMS - KEPT

SLOTS, GRP = 16, 4
GPR = SLOTS // GRP
ROUNDS = NE // SLOTS
GPP = GPR * ROUNDS
SHARE_FROM = 2
SHARE0_FROM = ROUNDS - 2
EARLY_V = 6
PER_TILE = 185

AT_CUM, AT_SOFT, AT_HGRN, AT_SOFT2, AT_CAUSAL, AT_STATE, AT_REC, AT_MIX, PAIR_STEP = 44, 50, 52, 56, 64, 68, 76, 90, 16
ODD_STEP, AT_OUT, OUT_STEP, HGRN_STEP, STATE_STEP = 5, 152, 9, 3, 2
ROUTE_ROWS = 6
FG_HEAD, ROPE_HEAD = 4, 6
SHARE0_POINTS = (5, 9, 13, 16)
ROUTE_STEPS = 17
GELU_M = 5

def at_mix(m):
    return AT_MIX + PAIR_STEP * (m // 2) + ODD_STEP * (m % 2)


assert at_mix(GELU_M) <= NE < at_mix(GELU_M + 1)

PI2_A = 6.28125
PI2_B = math.floor((2 * math.pi - PI2_A) * 2 ** 19) / 2 ** 19
PI2_C = 2 * math.pi - PI2_A - PI2_B
MAGIC = 1.5 * 2 ** 23


class Front:

    def __init__(self, name, t0, nt, item0, sem):
        self.name, self.t0, self.nt, self.item0 = name, t0, nt, item0
        self.n, self.nc = nt * P, 2 * nt
        self.xT_in = sem(f"{name}_xT_in")
        self.x_in = sem(f"{name}_x_in")
        self.proj_done = sem(f"{name}_proj_done")
        self.proj_out = sem(f"{name}_proj_out")
        self.rope_done = sem(f"{name}_rope_done")
        self.qk_turned = sem(f"{name}_qk_turned")
        self.qk_out = sem(f"{name}_qk_out")
        self.score_done = sem(f"{name}_score_done")
        self.score_out = sem(f"{name}_score_out")
        self.soft_arg = sem(f"{name}_soft_arg")
        self.soft_exp = sem(f"{name}_soft_exp")
        self.soft_den = sem(f"{name}_soft_den")
        self.soft_done = sem(f"{name}_soft_done")
        self.w_turned = sem(f"{name}_w_turned")
        self.w_outT = sem(f"{name}_w_outT")
        self.av_done = sem(f"{name}_av_done")
        self.av_out = sem(f"{name}_av_out")
        self.hgrn_ln = sem(f"{name}_hgrn_ln")
        self.fg_ready = sem(f"{name}_fg_ready")
        self.bcum_ready = sem(f"{name}_bcum_ready")
        self.hgrn_exp = sem(f"{name}_hgrn_exp")
        self.kq_ready = sem(f"{name}_kq_ready")
        self.vz_ready = sem(f"{name}_vz_ready")
        self.kend_turned = sem(f"{name}_kend_turned")
        self.kend_out = sem(f"{name}_kend_out")
        self.at_done = sem(f"{name}_at_done")
        self.at_out = sem(f"{name}_at_out")
        self.kv_done = sem(f"{name}_kv_done")
        self.state_ready = sem(f"{name}_state_ready")
        self.o_done = sem(f"{name}_o_done")
        self.o_out = sem(f"{name}_o_out")
        self.ms_ready = sem(f"{name}_ms_ready")
        self.rms_root = sem(f"{name}_rms_root")
        self.rec_ready = sem(f"{name}_rec_ready")
        self.rec_turned = sem(f"{name}_rec_turned")
        self.rec_out = sem(f"{name}_rec_out")
        self.gate_done = sem(f"{name}_gate_done")
        self.gate_ready = sem(f"{name}_gate_ready")
        self.mix_done = sem(f"{name}_mix_done")
        self.mix_out = sem(f"{name}_mix_out")
        self.y_done = sem(f"{name}_y_done")
        self.y_out = sem(f"{name}_y_out")
        self.var_ready = sem(f"{name}_var_ready")
        self.std_ready = sem(f"{name}_std_ready")
        self.x1_ready = sem(f"{name}_x1_ready")
        self.x1_turned = sem(f"{name}_x1_turned")
        self.x1_out = sem(f"{name}_x1_out")
        self.pq_done = sem(f"{name}_pq_done")
        self.pq_out = sem(f"{name}_pq_out")
        self.ks_done = sem(f"{name}_ks_done")
        self.ks_out = sem(f"{name}_ks_out")


def build(nc, x, xT, w_items, keysT, pos, inv_freq, sinks, lb_logits, norm_g,
          ln1, ln2, ident_d, causal_d, chunk_d, iota_d, u_rows, v_rows, out):
    with ExitStack() as ctx:
        def sb(name, shape, dt=F32):
            return ctx.enter_context(nc.sbuf_tensor(name, shape, dt))

        def sem(name):
            return ctx.enter_context(nc.semaphore(name))

        KB = 256
        arena = sb("arena", [P, 198 * KB])

        def view(kb, *dims, parts=P, dt=F32):
            n = 1
            for d in dims:
                n *= d
            a = arena[0:parts, int(kb * KB):int(kb * KB) + n]
            if dt != F32:
                a = a.bitcast(dt)
            if len(dims) == 1:
                return a
            names = "abcd"[:len(dims)]
            return a.rearrange(f"p ({' '.join(names)}) -> p {' '.join(names)}",
                               **{k: d for k, d in zip(names[1:], dims[1:])})

        rows = view(0, SLOTS, D)
        ring = view(64, RING, ITEMW)
        x1 = view(88, T, D)
        ln_gb = view(182, 2, D)
        acc = view(190, D)
        cur = view(194, SLOTS, dt=U32)
        eidx = view(194.125, T, NE, dt=U32)
        gexp = view(196.125, PH, TOPK)
        hid = view(196.625, NE)
        wv = view(197.125, NE)
        hid_r = view(197.625, SLOTS)
        gsum = view(197.75, PH)
        top = view(176, PH, 2, TOPK)
        topi = view(177, PH, 2, TOPK, dt=U32)
        topf = view(178, PH, 2, TOPK)
        sco = view(179, PH, TOPK)
        sci = view(179.5, PH, TOPK, dt=U32)
        half_i = view(177, 2, NE, dt=U32)
        half_f = view(180, 2, NE)
        e12 = view(181, 2, NE)
        ybuf = view(104, D)
        x1cur = view(108, D)
        diag = view(112, SLOTS, P)
        scur = view(120, 2 * PH, NK)
        cand = view(172, PH // 2, TOPK, TOPK)
        onehot = view(164, 2, NE // 2, TOPK)
        kept = [view(kb, ITEMW) for kb in (116, 124, 132, 167)]
        cand0, onehot0 = view(164, 1, TOPK, TOPK), view(165, 2, TOPK, TOPK)

        ident = sb("ident", [P, P])
        alphaI = sb("alphaI", [P, P])
        causal = sb("causal", [P, P], U32)
        chunk_mask = sb("chunk_mask", [P, (T - 1) * P])
        iota16 = sb("iota16", [P, TOPK])
        keys = sb("keys", [P, 2, NK])
        normg = sb("normg", [P, DV])
        state_in = sb("state_in", [P, HH, DV])
        k_last = sb("k_last", [HD, KVH, CH])
        v_last = sb("v_last", [P, KVH * HD])
        pos_i = sb("pos_i", [P, T], I32)
        pos_f = sb("pos_f", [P, T])
        freq = sb("freq", [P, HALF])
        sinkc = sb("sinkc", [P, PAIRS])
        lbl = sb("lbl", [P, 2, HH])
        lbm = sb("lbm", [P, HH])
        lbv = sb("lbv", [P, HH])
        omlb = sb("omlb", [P, HH])
        ang = sb("ang", [P, T, HALF])
        turns = sb("turns", [P, T, HALF])
        trig = sb("trig", [P, 2, T, HALF])
        mxb = sb("mx", [P, 3, NC, PAIRS])
        decayb = sb("decay", [P, HH, NC])
        rmsb = sb("rms", [P, T, HH])
        stats = sb("stats", [P, 2, 6])
        mv = sb("mv", [P, 2])
        rstd = sb("rstd", [P, 1])
        bank = ctx.enter_context(nc.psum_tensor("bank", [P, 8, 512], F32))

        A = Front("a", 0, 1, 0, sem)
        B = Front("b", 1, T - 1, RINGED, sem)
        consts_in = sem("consts_in")
        ln1_in = sem("ln1_in")
        ln2_in = sem("ln2_in")
        kept_in = [sem(f"kept_in{k}") for k in range(KEPT)]
        w_in = [sem(f"w_in{i}") for i in range(RING)]
        trig_arg = sem("trig_arg")
        trig_ready = sem("trig_ready")
        lb_arg = sem("lb_arg")
        lb_exp = sem("lb_exp")
        alpha_ready = sem("alpha_ready")
        step = sem("step")
        route_gate = sem("route_gate")
        idx_ready = sem("idx_ready")
        gexp_arg = sem("gexp_arg")
        gexp_done = sem("gexp_done")
        cur_ready = sem("cur_ready")
        pool_gate = sem("pool_gate")
        landed = [sem(f"landed{i}") for i in range(SLOTS)]
        u_used = sem("u_used")
        v_used = sem("v_used")
        v_shared = sem("v_shared")
        hid_ready = sem("hid_ready")
        gelu_done = sem("gelu_done")
        wv_ready = sem("wv_ready")
        act_gate = sem("act_gate")
        diag_ready = sem("diag_ready")
        acc_out = sem("acc_out")
        var2_ready = sem("var2_ready")
        std2_ready = sem("std2_ready")
        y2_ready = sem("y2_ready")
        y_free = sem("y_free")
        out_done = sem("out_done")

        A.tok = view(0, 1, TOKW)
        A.HQ, A.HF, A.KH = (view(7 + 2 * k, HH, A.n) for k in range(3))
        A.SQ, A.BC = view(13, 2, A.n), view(14, 2, A.n)
        A.rot = view(15, 4, 1, HEADS + KVH, HALF)
        A.qT = view(17, A.nc, HEADS, CH, parts=HD)
        A.SC = view(21, A.nc, PAIRS, P)
        A.PT = view(25, A.nc, PAIRS, P)
        A.attnT, A.recT = view(29, PAIRS, A.n), view(31, HH, A.n)
        A.kendT, A.AT, A.otok = view(33, 1, HH, DK), view(35, 1, HH, P), view(37, 1, HH, DV)
        A.ST = [view(39, HH, DV), view(41, HH, DV), state_in[:, :, :]]
        A.mixT = view(43, KC, A.n)
        A.sig = view(47, 2, 2, A.n)
        A.osq = view(49, HH, DV)
        A.act_in = view(190, KC, A.n)
        A.qTp = view(140, 2 * PH, A.n)
        A.s12 = view(156, 1, 2 * PH * NK)
        B.HQ, B.HF = view(92, HH, B.n), view(98, HH, B.n)
        B.act_in = view(104, KC, B.n)
        B.tok = view(116, B.nt, TOKW)
        B.qTp = view(116, 2 * PH, B.n)
        B.rot = view(140, 4, B.nt, HEADS + KVH, HALF)
        B.qT = view(140, B.nc, HEADS, CH, parts=HD)
        B.PT = view(140, B.nc, PAIRS, P)
        B.SC = view(152, B.nc, PAIRS, P)
        B.attnT = view(164, PAIRS, B.n)
        B.KH = view(170, HH, B.n)
        B.SQ, B.BC = view(176, 2, B.n), view(179, 2, B.n)
        B.kendT, B.AT = view(140, B.nt, HH, DK), view(146, B.nt, HH, P)
        B.ST = [state_in[:, :, :]] + [view(150 + 2 * k, HH, DV) for k in range(1, B.nc)]
        B.otok = view(98, B.nt, HH, DV)
        B.osq = view(179, HH, DV)
        B.recT = view(170, HH, B.n)
        B.mixT = view(140, KC, B.n)
        B.sig = view(152, 2, 2, B.n)
        B.s12 = view(140, B.nt, 2 * PH * NK)
        for F in (A, B):
            F.mx, F.snk, F.den = (mxb[:, k, 2 * F.t0:2 * F.t0 + F.nc, :] for k in range(3))
            F.decay = decayb[:, :, 2 * F.t0:2 * F.t0 + F.nc]
            F.rms = rmsb[:, F.t0:F.t0 + F.nt, :]
            F.x1 = x1[:, F.t0:F.t0 + F.nt, :]
            F.kT = F.tok[0:HD, :, K0 - KVH * P:K0].rearrange("p t (g k) -> p t g k", g=KVH)
            F.v_even, F.v_odd = F.tok[:, :, 0:KVH * HD], F.tok[:, :, KVH * HD:2 * KVH * HD]

        CONSTS = 11

        def out_units(F):
            return ([(k, t) for k in range(N_OUT - 2) for t in range(F.nt)]
                    + [(k, t) for t in range(F.nt) for k in range(N_OUT - 2, N_OUT)])

        def item(F, k):
            return kept[k] if k < KEPT else ring[:, (F.item0 + k - KEPT) % RING, :]

        def item_in(eng, F, k):
            if k < KEPT:
                eng.wait_ge(kept_in[k], 16)
            else:
                n = F.item0 + k - KEPT
                eng.wait_ge(w_in[n % RING], 16 * (n // RING + 1))

        def item_used(eng, F, k):
            if k < I_TOK:
                eng.wait_ge(F.proj_done, 2 * (k + 1))
            elif k < I_MIX:
                eng.wait_ge(F.proj_done, 2 * N_HQF + F.nt * (k - I_TOK + 1))
            elif k < I_OUT:
                pair, part = (k - I_MIX) // 3, (k - I_MIX) % 3
                if part < 2:
                    eng.wait_ge(F.gate_done, 2 * pair + part + 1)
                else:
                    eng.wait_ge(F.mix_done, 2 * pair + 2)
            elif k < I_WQ:
                eng.wait_ge(F.y_done, out_units(F).index((k - I_OUT, F.nt - 1)) + 1)
            else:
                eng.wait_ge(F.pq_done, 2 * (k - I_WQ + 1))

        class Chain:

            def __init__(self, eng):
                self.eng, self.n, self.dyn = eng, 0, []

            def value(self):
                v = self.n
                for turn, per in self.dyn:
                    v = turn * per + v
                return v

            def __call__(self, ins):
                ins.then_inc(step, 1)
                self.n += 1
                return ins

            def wait(self):
                self.eng.wait_ge(step, self.value())

            def gate(self):
                self.wait()
                self.eng.sem_inc(route_gate, 1)

            def enter(self, turn, per):
                self.dyn.append((turn, per))
                self.start = (self.n, per)

            def leave(self, start, times):
                _, per = self.dyn.pop()
                assert self.n - start == per, (self.n - start, per)
                self.n = start + per * times

        block = ctx.enter_context(nc.Block())

        @block.sync
        def _(sp):
            def load(F, k):
                if k < KEPT:
                    sp.dma_start(item(F, k), w_items[k]).then_inc(kept_in[k], 16)
                    return
                n = F.item0 + k - KEPT
                if n >= RING:
                    old = n - RING
                    item_used(sp, *((A, old + KEPT) if old < RINGED else (B, old - RINGED + KEPT)))
                sp.dma_start(item(F, k), w_items[k]).then_inc(w_in[n % RING], 16)

            def load_xT(F):
                sp.dma_start(F.act_in, xT.rearrange("(c p) t -> p c t", p=P)[:, :, F.t0 * P:(F.t0 + F.nt) * P]
                             ).then_inc(F.xT_in, 16)

            def load_x(F):
                sp.dma_start(F.x1, x.rearrange("(t p) d -> p t d", p=P)[:, F.t0:F.t0 + F.nt, :]).then_inc(F.x_in, 16)

            load_xT(A)
            load(A, 0)
            load(A, 1)
            for dst, src in ((ident[:, :], ident_d), (causal[:, :], causal_d), (chunk_mask[:, :], chunk_d),
                             (iota16[:, :], iota_d), (keys[:, :, :], keysT), (pos_i[:, :], pos),
                             (lbl[:, :, :], lb_logits), (freq[:, :], inv_freq.partition_broadcast(P)),
                             (normg[:, :], norm_g.partition_broadcast(P))):
                sp.dma_start(dst, src).then_inc(consts_in, 16)
            for hh in range(2):
                sp.dma_start(sinkc[CH * hh:CH * hh + CH, :], sinks[hh, :].partition_broadcast(CH)).then_inc(consts_in, 16)
            for k in range(2, I_MIX):
                load(A, k)
            load_x(A)
            load_xT(B)
            for k in range(2):
                sp.dma_start(ln_gb[:, k, :], ln1[k, :].partition_broadcast(P)).then_inc(ln1_in, 16)
            for k in range(I_MIX, ITEMS):
                load(A, k)
            for k in range(KEPT, ITEMS):
                load(B, k)
                if k == I_MIX + RING:
                    sp.wait_ge(B.rec_turned, B.nt)
                    load_x(B)
            sp.wait_ge(B.x1_ready, B.nt)
            for k in range(2):
                sp.dma_start(ln_gb[:, k, :], ln2[k, :].partition_broadcast(P)).then_inc(ln2_in, 16)
            sp.sem_inc(y_free, 1)
            with sp.Fori(0, T) as t:
                sp.wait_ge(y2_ready, t + 1)
                sp.dma_start(out[bass.ds(t * P, P), :], ybuf).then_inc(out_done, 16)
                sp.wait_ge(out_done, 16 * (t + 1))
                sp.sem_inc(y_free, 1)
            sp.wait_ge(out_done, 16 * T)

        @block.tensor
        def _(pe):
            mm = nc.tensor.matmul
            turn = nc.tensor.transpose

            def front(F, other=None):
                n, nt = F.n, F.nt
                pe.wait_ge(F.xT_in, 16)
                if other is not None:
                    pe.wait_ge(other.pq_out, 2 * PH)

                for b in range(2 * N_HQF):
                    item_in(pe, F, b // 2)
                    w = item(F, b // 2).rearrange("p (c n) -> p c n", c=KC)
                    if b >= 4:
                        pe.wait_ge(F.proj_out, b - 3)
                    for c in range(KC):
                        last = mm(bank[:, b % 4, 0:n], w[:, c, b % 2 * P:(b % 2 + 1) * P], F.act_in[:, c, :],
                                  start=c == 0, stop=c == KC - 1)
                    last.then_inc(F.proj_done, 1)

                def project_tok(k):
                    item_in(pe, F, I_TOK + k)
                    w = item(F, I_TOK + k).rearrange("p (c n) -> p c n", c=KC)
                    for t in range(nt):
                        b = 2 * N_HQF + k * nt + t
                        pe.wait_ge(F.proj_out, b - 3)
                        for c in range(KC):
                            last = mm(bank[:, b % 4, 0:TW], F.act_in[:, c, t * P:(t + 1) * P], w[:, c, :],
                                      start=c == 0, stop=c == KC - 1)
                        last.then_inc(F.proj_done, 1)

                for k in range(TOK_EARLY):
                    project_tok(k)

                pe.wait_ge(consts_in, 16 * CONSTS)
                pe.wait_ge(F.rope_done, 1)
                if other is not None:
                    pe.wait_ge(other.ks_out, PH)
                for t in range(nt):
                    for part in range(3):
                        u = 3 * t + part
                        if u >= 4:
                            pe.wait_ge(F.qk_out, u - 3)
                        for k in range(4 if part < 2 else 2):
                            h = 4 * part + k
                            last = turn(bank[0:HD, 4 + u % 4, k * P:(k + 1) * P],
                                        F.tok[:, t, h * HD:(h + 1) * HD], ident[:, :])
                        last.then_inc(F.qk_turned, 1)

                pe.wait_ge(F.qk_out, 3 * nt)
                for c in range(F.nc):
                    if c >= 4:
                        pe.wait_ge(F.score_out, c - 3)
                    for j in range(PAIRS):
                        g = j // (PAIRS // KVH)
                        q = F.qT[:, c, 2 * j:2 * j + 2, :]
                        o = bank[:, 4 + c % 4, j * P:(j + 1) * P]
                        if c % 2:
                            last = mm(o, q, F.kT[:, c // 2, g, :], start=True, stop=True)
                        else:
                            last = mm(o[:, 0:CH], q, F.kT[:, c // 2, g, 0:CH], start=True, stop=True)
                            if c or F.t0:
                                before = F.kT[:, c // 2 - 1, g, CH:P] if c else k_last[:, g, :]
                                last = mm(o[:, CH:P], q, before, start=True, stop=True)
                    last.then_inc(F.score_done, 1)

                for k in range(TOK_EARLY, N_TOK):
                    project_tok(k)

                def turn_weights(c):
                    pe.wait_ge(F.soft_done, c + 1)
                    if c >= 2:
                        pe.wait_ge(F.w_outT, c - 1)
                    for j in range(PAIRS):
                        last = turn(bank[:, 4 + c % 2, j * P:(j + 1) * P], F.SC[:, c, j, :], ident[:, :])
                    last.then_inc(F.w_turned, 1)

                def times_v(c):
                    pe.wait_ge(F.w_outT, c + 1)
                    if c >= 2:
                        pe.wait_ge(F.av_out, c - 1)
                    for j in range(PAIRS):
                        g = j // (PAIRS // KVH)
                        vc = slice(V0 + g * HD, V0 + (g + 1) * HD)
                        vz = slice(g * HD, (g + 1) * HD)
                        for hh in range(2):
                            o = bank[hh * HD:(hh + 1) * HD, 6 + c % 2, j * CH:(j + 1) * CH]
                            p = F.PT[:, c, j, hh * CH:(hh + 1) * CH]
                            if c % 2:
                                last = mm(o, F.tok[:, c // 2, vc], p, start=True, stop=True)
                            else:
                                first = c == 0 and F.t0 == 0
                                last = mm(o, F.v_even[:, c // 2, vz], p, start=True, stop=first)
                                if not first:
                                    before = F.v_odd[:, c // 2 - 1, vz] if c else v_last[:, vz]
                                    last = mm(o, before, p, start=False, stop=True)
                    last.then_inc(F.av_done, 1)

                pe.wait_ge(F.vz_ready, 1)
                turn_weights(0)
                for c in range(F.nc):
                    if c + 1 < F.nc:
                        turn_weights(c + 1)
                    times_v(c)

                pe.wait_ge(F.kq_ready, 1)
                pe.wait_ge(F.av_out, F.nc)
                for t in range(nt):
                    tokens = slice(t * P, (t + 1) * P)
                    if t >= 2:
                        pe.wait_ge(F.kend_out, t - 1)
                    for h in range(HH):
                        last = turn(bank[:, 4 + t % 2, h * P:(h + 1) * P], F.HF[:, h, tokens], ident[:, :])
                    last.then_inc(F.kend_turned, 1)
                    if t >= 2:
                        pe.wait_ge(F.at_out, t - 1)
                    for h in range(HH):
                        last = mm(bank[:, 6 + t % 2, h * P:(h + 1) * P], F.KH[:, h, tokens], F.HQ[:, h, tokens],
                                  start=True, stop=True)
                    last.then_inc(F.at_done, 1)

                states = F.nc if F.t0 == 0 else F.nc - 1

                def chunk_kv(c):
                    if c >= states:
                        return
                    t, cc = c // 2, c % 2
                    pe.wait_ge(F.kend_out, t + 1)
                    if c >= 2:
                        pe.wait_ge(F.state_ready, c)
                    for h in range(HH):
                        last = mm(bank[:, c % 2, h * DV:(h + 1) * DV], F.kendT[cc * CH:(cc + 1) * CH, t, h, :],
                                  F.tok[cc * CH:(cc + 1) * CH, t, I0 + h * DV:I0 + (h + 1) * DV], start=True, stop=True)
                    last.then_inc(F.kv_done, 1)

                def tile_out(t):
                    pe.wait_ge(F.at_out, t + 1)
                    if t >= 2:
                        pe.wait_ge(F.o_out, t - 1)
                    pe.wait_ge(F.state_ready, 2 * t + 2)
                    for h in range(HH):
                        hv = slice(h * DV, (h + 1) * DV)
                        mm(bank[:, 2 + t % 2, hv], F.AT[:, t, h, :], F.tok[:, t, I0 + h * DV:I0 + (h + 1) * DV],
                           start=True, stop=False, skip_group_check=True)
                        for cc in range(2):
                            c = 2 * t + cc
                            last = mm(bank[cc * CH:(cc + 1) * CH, 2 + t % 2, hv], F.HQ[:, h, c * CH:(c + 1) * CH],
                                      F.ST[c][:, h, :], start=False, stop=True, skip_group_check=True)
                    last.then_inc(F.o_done, 1)

                def turn_rec(t):
                    pe.wait_ge(F.rec_ready, t + 1)
                    if t >= 2:
                        pe.wait_ge(F.rec_out, t - 1)
                    for h in range(HH):
                        last = turn(bank[:, 6 + t % 2, h * P:(h + 1) * P], F.otok[:, t, h, :], ident[:, :])
                    last.then_inc(F.rec_turned, 1)

                pe.wait_ge(F.proj_out, 2 * N_HQF + N_TOK * nt)
                chunk_kv(0)
                for t in range(nt):
                    chunk_kv(2 * t + 1)
                    tile_out(t)
                    chunk_kv(2 * t + 2)

                def gates(m):
                    k = I_MIX + 3 * (m // 2) + m % 2
                    item_in(pe, F, k)
                    w = item(F, k).rearrange("p (c n) -> p c n", n=P)
                    if m >= 2:
                        pe.wait_ge(F.mix_out, m - 1)
                    b = 4 * (m % 2)
                    for g in range(2):
                        for c in range(KC):
                            last = mm(bank[:, b + g, 0:n], w[:, g * KC + c, :], F.act_in[:, c, :],
                                      start=c == 0, stop=c == KC - 1)
                    last.then_inc(F.gate_done, 1)

                def branches(m):
                    k = I_MIX + 3 * (m // 2) + 2
                    item_in(pe, F, k)
                    w = item(F, k).rearrange("p (m c n) -> p m c n", m=2, n=P)
                    b = 4 * (m % 2)
                    for j in range(PAIRS):
                        mm(bank[:, b + 2, 0:n], w[:, m % 2, j, :], F.attnT[:, j, :], start=j == 0, stop=j == PAIRS - 1)
                    for h in range(HH):
                        last = mm(bank[:, b + 3, 0:n], w[:, m % 2, PAIRS + h, :], F.recT[:, h, :],
                                  start=h == 0, stop=h == HH - 1)
                    last.then_inc(F.mix_done, 1)

                pe.wait_ge(F.state_ready, states + 1)
                for m in range(0, KC, 2):
                    gates(m)
                    gates(m + 1)
                    if m == 0:
                        for t in range(nt):
                            turn_rec(t)
                        pe.wait_ge(F.rec_out, nt)
                    branches(m)
                    branches(m + 1)

                pe.wait_ge(F.mix_out, KC)
                for u, (k, t) in enumerate(out_units(F)):
                    item_in(pe, F, I_OUT + k)
                    w = item(F, I_OUT + k).rearrange("p (c n) -> p c n", c=KC)
                    if u >= 4:
                        pe.wait_ge(F.y_out, u - 3)
                    for c in range(KC):
                        last = mm(bank[:, u % 4, 0:TW], F.mixT[:, c, t * P:(t + 1) * P], w[:, c, :],
                                  start=c == 0, stop=c == KC - 1)
                    last.then_inc(F.y_done, 1)

                for t in range(nt):
                    pe.wait_ge(F.x1_ready, t + 1)
                    for half in range(2):
                        u = 2 * t + half
                        if u >= 4:
                            pe.wait_ge(F.x1_out, u - 3)
                        for k in range(4):
                            c = 4 * half + k
                            last = turn(bank[:, 4 + u % 4, k * P:(k + 1) * P], F.x1[:, t, c * P:(c + 1) * P], ident[:, :])
                        last.then_inc(F.x1_turned, 1)

                pe.wait_ge(F.x1_out, 2 * nt)
                pe.wait_ge(F.y_out, N_OUT * nt)

                def key_scores(h):
                    pe.wait_ge(F.pq_out, 2 * h + 2)
                    for t in range(nt):
                        u = h * nt + t
                        if u >= 4:
                            pe.wait_ge(F.ks_out, u - 3)
                        for half in range(2):
                            last = mm(bank[:, 4 + u % 4, half * NK:(half + 1) * NK],
                                      F.qTp[:, 2 * h + half, t * P:(t + 1) * P], keys[:, half, :], start=True, stop=True)
                        last.then_inc(F.ks_done, 1)

                for h in range(PH):
                    item_in(pe, F, I_WQ + h)
                    w = item(F, I_WQ + h).rearrange("p (c n) -> p c n", c=KC)
                    for half in range(2):
                        b = 2 * h + half
                        if b >= 4:
                            pe.wait_ge(F.pq_out, b - 3)
                        for c in range(KC):
                            last = mm(bank[:, b % 4, 0:n], w[:, c, half * P:(half + 1) * P], F.act_in[:, c, :],
                                      start=c == 0, stop=c == KC - 1)
                        last.then_inc(F.pq_done, 1)
                    if h != 1:
                        key_scores(max(h - 1, 0))
                key_scores(PH - 1)

            front(A)
            front(B, A)

            pe.wait_ge(alpha_ready, 1)
            pe.wait_ge(B.ks_out, PH * B.nt)
            pe.wait_ge(B.pq_out, 2 * PH)

            def residual(t):
                pe.wait_ge(acc_out, t + 1)
                for n in range(2):
                    mm(bank[:, n, :], alphaI[:, :], x1.rearrange("p t d -> p (t d)")[:, bass.ds(t * D + n * 512, 512)],
                       start=True, stop=False, skip_group_check=True)

            def v_round(t, i, shared):
                mine = [s for s in range(SLOTS) if not (shared and s % GRP == GRP - 1)]
                for s in mine:
                    if s % GRP == 0:
                        pe.wait_ge(diag_ready, GPP * t + GPR * (i - EARLY_V) + s // GRP + 1)
                    pe.wait_ge(landed[s], 16 * (2 * ROUNDS * t + ROUNDS + i + 1))
                    mm(bank[:, 0, :], diag[:, s, :], rows[:, s, 0:512], start=False, stop=False, skip_group_check=True)
                    last = mm(bank[:, 1, :], diag[:, s, :], rows[:, s, 512:D], start=False, stop=False,
                              skip_group_check=True)
                    if s % GRP == GRP - 1 - shared:
                        last.then_inc(v_used, 1)

            residual(0)
            pe.wait_ge(v_used, GPR + GPR * EARLY_V)
            for i in range(EARLY_V, ROUNDS):
                v_round(0, i, i >= SHARE0_FROM)
            with pe.Fori(1, T) as t:
                residual(t)
                with pe.Fori(0, SHARE_FROM) as i:
                    v_round(t, i, False)
                with pe.Fori(SHARE_FROM, ROUNDS) as i:
                    v_round(t, i, True)

        @block.scalar
        def _(act):
            fn = nc.scalar.activation

            def front(F):
                n, nt = F.n, F.nt
                for b in range(2 * N_HQF):
                    act.wait_ge(F.proj_done, b + 1)
                    dst, f = (F.HF, ACT.Sigmoid) if b < 4 else (F.HQ, ACT.Silu)
                    fn(dst[:, b % 4, :], bank[:, b % 4, 0:n], f).then_inc(F.proj_out, 1)

                def copy_tok(k):
                    for t in range(nt):
                        b = 2 * N_HQF + k * nt + t
                        act.wait_ge(F.proj_done, b + 1)
                        fn(F.tok[:, t, k * TW:(k + 1) * TW], bank[:, b % 4, 0:TW],
                           ACT.Copy if k * TW < G0 else ACT.Silu).then_inc(F.proj_out, 1)

                if F is A:
                    act.wait_ge(lb_arg, 1)
                    fn(lbl[:, :, :], lbl[:, :, :], ACT.Exp).then_inc(lb_exp, 1)
                    act.wait_ge(trig_arg, 1)
                    fn(trig[:, :, :, :], trig[:, :, :, :], ACT.Sin).then_inc(trig_ready, 1)
                for k in range(TOK_EARLY):
                    copy_tok(k)


                for t in range(nt):
                    for part in range(3):
                        u = 3 * t + part
                        act.wait_ge(F.qk_turned, u + 1)
                        src = bank[0:HD, 4 + u % 4, :]
                        if part < 2:
                            src = src.rearrange("p (h c q) -> p h c q", h=4, c=2)
                            dst = F.qT[:, 2 * t:2 * t + 2, 4 * part:4 * part + 4, :].rearrange("p c h q -> p h c q")
                        else:
                            src = src[:, 0:KVH * P].rearrange("p (h q) -> p h q", h=KVH)
                            dst = F.kT[:, t, :, :]
                        fn(dst, src, ACT.Copy).then_inc(F.qk_out, 1)
                for h in range(HH):
                    act.wait_ge(F.fg_ready, h + 1)
                    fn(F.HF[:, h, :], F.HF[:, h, :], ACT.Ln).then_inc(F.hgrn_ln, 1)
                if F is B:
                    act.wait_ge(gexp_arg, 1)
                    fn(gexp, gexp, ACT.Exp).then_inc(gexp_done, 1)
                for c in range(F.nc):
                    act.wait_ge(F.score_done, c + 1)
                    w = CH if c == 0 and F is A else P
                    fn(F.SC[:, c, :, 0:w], bank[:, 4 + c % 4, :].rearrange("p (j k) -> p j k", j=PAIRS)[:, :, 0:w],
                       ACT.Copy, scale=SCALE).then_inc(F.score_out, 1)
                def decays(h):
                    act.wait_ge(F.bcum_ready, h + 1)
                    fn(F.SQ[:, h % 2, :], F.BC[:, h % 2, :], ACT.Exp).then_inc(F.hgrn_exp, 1)
                    fn(F.HF[:, h, :], F.HF[:, h, :], ACT.Exp).then_inc(F.hgrn_exp, 1)
                    act.wait_ge(F.hgrn_exp, 3 * h + 2)
                    fn(F.BC[:, h % 2, :], F.BC[:, h % 2, :], ACT.Exp, scale=-1.0).then_inc(F.hgrn_exp, 1)

                decays(0)
                decays(1)
                act.wait_ge(F.soft_arg, 1)
                fn(F.snk, F.snk, ACT.Exp)
                for c in range(F.nc):
                    for j in range(PAIRS):
                        last = fn(F.SC[:, c, j, :], F.SC[:, c, j, :], ACT.Exp, bias=F.mx[:, c, j:j + 1])
                    last.then_inc(F.soft_exp, 1)
                copy_tok(TOK_EARLY)
                decays(2)
                decays(3)
                for c in range(F.nc):
                    act.wait_ge(F.soft_den, c // (F.nc // 2) + 1)
                    for j in range(PAIRS):
                        last = fn(F.SC[:, c, j, :], F.SC[:, c, j, :], ACT.Copy, scale=F.den[:, c, j:j + 1])
                    last.then_inc(F.soft_done, 1)
                for k in range(TOK_EARLY + 1, N_TOK):
                    copy_tok(k)

                def copy_wT(c):
                    act.wait_ge(F.w_turned, c + 1)
                    fn(F.PT[:, c, :, :], bank[:, 4 + c % 2, :].rearrange("p (j k) -> p j k", j=PAIRS),
                       ACT.Copy).then_inc(F.w_outT, 1)

                copy_wT(0)
                for c in range(F.nc):
                    if c + 1 < F.nc:
                        copy_wT(c + 1)
                    act.wait_ge(F.av_done, c + 1)
                    fn(F.attnT[:, :, c * CH:(c + 1) * CH],
                       bank[:, 6 + c % 2, 0:PAIRS * CH].rearrange("p (j q) -> p j q", j=PAIRS), ACT.Copy).then_inc(F.av_out, 1)
                for t in range(nt):
                    act.wait_ge(F.kend_turned, t + 1)
                    fn(F.kendT[:, t, :, :], bank[:, 4 + t % 2, :].rearrange("p (h k) -> p h k", h=HH),
                       ACT.Copy).then_inc(F.kend_out, 1)

                for t in range(nt):
                    act.wait_ge(F.o_done, t + 1)
                    fn(F.otok[:, t, :, :], bank[:, 2 + t % 2, :].rearrange("p (h e) -> p h e", h=HH), ACT.Copy).then_inc(F.o_out, 1)
                for t in range(nt):
                    act.wait_ge(F.ms_ready, t + 1)
                    fn(F.rms[:, t, :], F.rms[:, t, :], ACT.Sqrt).then_inc(F.rms_root, 1)
                for m in range(KC):
                    if m == 2:
                        for t in range(nt):
                            act.wait_ge(F.rec_turned, t + 1)
                            fn(F.recT[:, :, t * P:(t + 1) * P], bank[:, 6 + t % 2, :].rearrange("p (h k) -> p h k", h=HH),
                               ACT.Copy).then_inc(F.rec_out, 1)
                    act.wait_ge(F.gate_done, m + 1)
                    if m >= 2:
                        act.wait_ge(F.mix_out, m - 1)
                    for k in range(2):
                        fn(F.sig[:, m % 2, k, :], bank[:, 4 * (m % 2) + k, 0:n], ACT.Sigmoid).then_inc(F.gate_ready, 1)
                    if F is B and m == GELU_M:
                        act.wait_ge(hid_ready, 1)
                        fn(hid, hid, ACT.Gelu).then_inc(gelu_done, 1)

                def copy_x1(u):
                    act.wait_ge(F.x1_turned, u + 1)
                    fn(F.act_in[:, u % 2 * 4:u % 2 * 4 + 4, u // 2 * P:(u // 2 + 1) * P],
                       bank[:, 4 + u % 4, :].rearrange("p (c k) -> p c k", c=4), ACT.Copy).then_inc(F.x1_out, 1)

                for t in range(nt):
                    act.wait_ge(F.var_ready, t + 1)
                    fn(rstd[:, :], rstd[:, :], ACT.Sqrt).then_inc(F.std_ready, 1)
                for u in range(2 * nt):
                    copy_x1(u)

                def copy_scores(h):
                    for t in range(nt):
                        u = h * nt + t
                        act.wait_ge(F.ks_done, u + 1)
                        fn(F.s12[:, t, h * 2 * NK:(h + 1) * 2 * NK], bank[:, 4 + u % 4, 0:2 * NK], ACT.Copy).then_inc(F.ks_out, 1)

                for h in range(PH):
                    for b in (2 * h, 2 * h + 1):
                        act.wait_ge(F.pq_done, b + 1)
                        fn(F.qTp[:, b, :], bank[:, b % 4, 0:n], ACT.Copy).then_inc(F.pq_out, 1)
                    if h != 1:
                        copy_scores(max(h - 1, 0))
                copy_scores(PH - 1)

            front(A)
            front(B)

            def diagonals(t, i, shared):
                for g in range(GPR):
                    act.wait_ge(v_used, GPP * t + GPR * i + g + 1)
                    act.sem_inc(act_gate, 1)
                    for k in range(GRP - shared):
                        s = g * GRP + k
                        last = fn(diag[:, s, :], ident[:, :], ACT.Copy, scale=wv[:, bass.ds(i * SLOTS + s, 1)])
                    last.then_inc(diag_ready, 1)

            act.wait_ge(wv_ready, 1)
            for i in range(EARLY_V, ROUNDS):
                diagonals(0, i, i >= SHARE0_FROM)
            with act.Fori(1, T) as t:
                act.wait_ge(gexp_arg, t + 1)
                fn(gexp, gexp, ACT.Exp).then_inc(gexp_done, 1)
                act.wait_ge(hid_ready, t + 1)
                fn(hid, hid, ACT.Gelu).then_inc(gelu_done, 1)
                act.wait_ge(var2_ready, t)
                fn(rstd[:, :], rstd[:, :], ACT.Sqrt).then_inc(std2_ready, 1)
                act.wait_ge(wv_ready, t + 1)
                act.sem_inc(act_gate, 1)
                with act.Fori(0, SHARE_FROM) as i:
                    diagonals(t, i, False)
                with act.Fori(SHARE_FROM, ROUNDS) as i:
                    diagonals(t, i, True)
            act.wait_ge(var2_ready, T)
            fn(rstd[:, :], rstd[:, :], ACT.Sqrt).then_inc(std2_ready, 1)

        @block.vector
        def _(dve):
            v = nc.vector
            ch = Chain(dve)

            def steps(*ins, fill=None):
                for x in ins:
                    ch(x())
                if fill:
                    fill()
                ch.wait()

            dve.wait_ge(consts_in, 16 * CONSTS)
            steps(lambda: v.tensor_tensor(lbm[:, :], lbl[:, 0, :], lbl[:, 1, :], ALU.max),
                  lambda: v.tensor_copy(pos_f[:, :], pos_i[:, :]),
                  lambda: v.tensor_scalar(alphaI[:, :], ident[:, :], ALPHA, None, ALU.mult),
                  lambda: v.memset(v_last[0:CH, :], 0.0))
            dve.sem_inc(alpha_ready, 1)
            v.tensor_tensor(lbl[:, :, :], lbl[:, :, :], lbm[:, :].unsqueeze(1).to_broadcast([P, 2, HH]), ALU.subtract).then_inc(lb_arg, 1)
            steps(lambda: v.tensor_tensor(ang[:, :, :], pos_f[:, :].unsqueeze(2).to_broadcast([P, T, HALF]),
                                          freq[:, :].unsqueeze(1).to_broadcast([P, T, HALF]), ALU.mult))
            steps(lambda: v.tensor_scalar(turns[:, :, :], ang[:, :, :], 1.0 / (2 * math.pi), None, ALU.mult))
            steps(lambda: v.tensor_scalar(turns[:, :, :], turns[:, :, :], MAGIC, None, ALU.add))
            steps(lambda: v.tensor_scalar(turns[:, :, :], turns[:, :, :], MAGIC, None, ALU.subtract))
            for part in (PI2_A, PI2_B, PI2_C):
                steps(lambda: v.scalar_tensor_tensor(out=ang[:, :, :], in0=turns[:, :, :], scalar=-part,
                                                     in1=ang[:, :, :], op0=ALU.mult, op1=ALU.add))
            steps(lambda: v.tensor_scalar(trig[:, 1, :, :], ang[:, :, :], 3.1415925, -3.1415925, ALU.min, ALU.max))
            steps(lambda: v.tensor_scalar(trig[:, 0, :, :], trig[:, 1, :, :], -1.0, None, ALU.mult))
            steps(lambda: v.tensor_tensor(trig[:, 0, :, :], trig[:, 0, :, :], trig[:, 1, :, :], ALU.min))
            steps(lambda: v.tensor_scalar(trig[:, 0, :, :], trig[:, 0, :, :], math.pi / 2, None, ALU.add))
            dve.sem_inc(trig_arg, 1)
            dve.wait_ge(lb_exp, 1)
            steps(lambda: v.tensor_tensor(lbm[:, :], lbl[:, 0, :], lbl[:, 1, :], ALU.add))
            steps(lambda: v.reciprocal(lbm[:, :], lbm[:, :]))
            steps(lambda: v.tensor_tensor(lbv[:, :], lbl[:, 0, :], lbm[:, :], ALU.mult))
            steps(lambda: v.tensor_scalar(omlb[:, :], lbv[:, :], -1.0, 1.0, ALU.mult, ALU.add))

            def rows_until(q):
                while done[0] < q:
                    k = done[0]
                    s = k % SLOTS
                    if k < NE:
                        dve.wait_ge(landed[s], 16 * (k // SLOTS + 1))
                        last = v.tensor_tensor_reduce(rows[:, s, :], rows[:, s, :], x1[:, 0, :], 1.0, 0.0,
                                                      ALU.mult, ALU.add, hid[:, k:k + 1])
                        if s % GRP == GRP - 1:
                            last.then_inc(u_used, 1)
                    else:
                        if k == NE:
                            dve.wait_ge(u_used, GPP)
                            dve.sem_inc(hid_ready, 1)
                            weights(0)
                            dve.sem_inc(v_shared, GPR * SHARE0_FROM)
                            steps(lambda: v.memset(acc, 0.0))
                        j = k - NE
                        dve.wait_ge(landed[s], 16 * (k // SLOTS + 1))
                        ch.wait()
                        ch(v.scalar_tensor_tensor(out=acc, in0=rows[:, s, :], scalar=wv[:, j:j + 1], in1=acc,
                                                  op0=ALU.mult, op1=ALU.add))
                        if s % GRP == GRP - 1:
                            ch.wait()
                            dve.sem_inc(v_used, 1)
                    done[0] += 1

            done = [0]

            def forget_gates(F):
                dve.wait_ge(F.proj_out, 4 if F is A else 2 * KEPT)
                for h in range(HH):
                    ch(v.tensor_scalar(F.HF[:, h, :], F.HF[:, h, :], omlb[:, h:h + 1], lbv[:, h:h + 1], ALU.mult, ALU.add))
                ch.wait()
                for h in range(HH):
                    v.tensor_scalar(F.KH[:, h, :], F.HF[:, h, :], -1.0, 1.0, ALU.mult, ALU.add).then_inc(F.fg_ready, 1)

            def rotate(F):
                nt = F.nt
                dve.wait_ge(trig_ready, 1)
                dve.wait_ge(F.proj_out, 2 * N_HQF + 3 * nt)
                heads = F.tok[:, :, 0:V0].rearrange("p t (h d) -> p t h d", d=HD)
                first, second = heads[:, :, :, 0:HALF], heads[:, :, :, HALF:ROT]
                full = [P, nt, HEADS + KVH, HALF]
                cos = trig[:, 0, F.t0:F.t0 + nt, :].unsqueeze(2).to_broadcast(full)
                sin = trig[:, 1, F.t0:F.t0 + nt, :].unsqueeze(2).to_broadcast(full)
                for k in range(4):
                    ch(v.tensor_tensor(F.rot[:, k, :, :, :], (first, second, second, first)[k],
                                       (cos, sin, cos, sin)[k], ALU.mult))
                ch.wait()
                ch(v.tensor_tensor(first, F.rot[:, 0, :, :, :], F.rot[:, 1, :, :, :], ALU.subtract))
                v.tensor_tensor(second, F.rot[:, 2, :, :, :], F.rot[:, 3, :, :, :], ALU.add).then_inc(F.rope_done, 1)

            def front(F, rows_until):
                n, nt, nch = F.n, F.nt, F.nc
                rows_until(AT_CUM)

                def cumulate(h):
                    dve.wait_ge(F.hgrn_ln, h + 1)
                    steps(lambda: v.tensor_tensor_scan(F.BC[:, h % 2, :], chunk_mask[:, 0:n], F.HF[:, h, :], 0.0,
                                                       ALU.mult, ALU.add))
                    bc, hf = (z.rearrange("p (c l) -> p c l", l=CH) for z in (F.BC[:, h % 2, :], F.HF[:, h, :]))
                    v.tensor_tensor(hf, bc[:, :, CH - 1:CH].to_broadcast([P, nch, CH]), bc,
                                    ALU.subtract).then_inc(F.bcum_ready, 1)

                def decayed(h):
                    dve.wait_ge(F.hgrn_exp, 3 * h + 1)
                    ch(v.tensor_tensor(F.HQ[:, h, :], F.HQ[:, h, :], F.SQ[:, h % 2, :], ALU.mult))
                    ch(v.tensor_copy(F.decay[:, h, :], F.SQ[:, h % 2, :].rearrange("p (c l) -> p c l", l=CH)[:, :, CH - 1]))
                    dve.wait_ge(F.hgrn_exp, 3 * h + 2)
                    ch(v.tensor_tensor(F.HF[:, h, :], F.HF[:, h, :], F.KH[:, h, :], ALU.mult))
                    ch.wait()
                    dve.wait_ge(F.hgrn_exp, 3 * h + 3)
                    steps(lambda: v.tensor_tensor(F.KH[:, h, :], F.KH[:, h, :], F.BC[:, h % 2, :], ALU.mult))

                dve.wait_ge(F.proj_out, 2 * N_HQF)
                cumulate(0)
                cumulate(1)

                rows_until(AT_SOFT)
                if F is A:
                    steps(lambda: v.memset(F.SC[:, 0, :, CH:P], NEG))
                dve.wait_ge(F.score_out, nch)
                sink = sinkc[:, :].unsqueeze(1).to_broadcast([P, nch, PAIRS])
                steps(lambda: v.tensor_reduce(F.mx, F.SC, AX_X, ALU.max))
                steps(lambda: v.tensor_tensor(F.mx, F.mx, sink, ALU.max))
                steps(lambda: v.tensor_tensor(F.snk, sink, F.mx, ALU.subtract),
                      lambda: v.tensor_scalar(F.mx, F.mx, -1.0, None, ALU.mult))
                dve.sem_inc(F.soft_arg, 1)
                steps(lambda: v.memset(F.v_even[CH:P, :, :], 0.0),
                      lambda: v.memset(F.v_odd[0:CH, :, :], 0.0),
                      lambda: v.tensor_copy(F.v_even[0:CH, :, :], F.tok[0:CH, :, V0:I0]),
                      lambda: v.tensor_copy(F.v_odd[CH:P, :, :], F.tok[CH:P, :, V0:I0]))
                if F is A:
                    steps(lambda: v.tensor_copy(v_last[CH:P, :], F.tok[CH:P, 0, V0:I0]),
                          lambda: v.tensor_copy(k_last[:, :, :], F.kT[:, 0, :, CH:P]))
                dve.sem_inc(F.vz_ready, 1)

                for h in range(2):
                    decayed(h)
                    cumulate(h + 2)
                    rows_until(AT_HGRN + HGRN_STEP * h)

                rows_until(AT_SOFT2)
                for half in range(2):
                    cs = slice(half * nch // 2, (half + 1) * nch // 2)
                    dve.wait_ge(F.soft_exp, cs.stop)
                    steps(lambda: v.tensor_reduce(F.den[:, cs, :], F.SC[:, cs, :, :], AX_X, ALU.add))
                    steps(lambda: v.tensor_tensor(F.den[:, cs, :], F.den[:, cs, :], F.snk[:, cs, :], ALU.add))
                    v.reciprocal(F.den[:, cs, :], F.den[:, cs, :]).then_inc(F.soft_den, 1)
                decayed(2)
                decayed(3)
                dve.sem_inc(F.kq_ready, 1)

                rows_until(AT_CAUSAL)
                dve.wait_ge(F.proj_out, 2 * N_HQF + N_TOK * nt)
                gate = F.tok[:, :, G0:G0 + HH * DV].rearrange("p t (h e) -> p t h e", h=HH)
                steps(lambda: v.tensor_tensor(gate, gate, normg[:, :].unsqueeze(1).unsqueeze(1).to_broadcast([P, nt, HH, DV]),
                                              ALU.mult))
                dve.wait_ge(F.w_outT, nch)
                dve.wait_ge(F.av_done, nch)
                steps(lambda: v.memset(F.AT, 0.0))
                if F is A:
                    steps(lambda: v.memset(F.ST[0], 0.0))
                for t in range(nt):
                    dve.wait_ge(F.at_done, t + 1)
                    v.copy_predicated(F.AT[:, t, :, :], causal[:, :].unsqueeze(1).to_broadcast([P, HH, P]),
                                      bank[:, 6 + t % 2, :].rearrange("p (h l) -> p h l", h=HH)).then_inc(F.at_out, 1)

                def state(c):
                    dve.wait_ge(F.kv_done, c + 1)
                    dve.wait_ge(F.state_ready, c + 1)
                    for h in range(HH):
                        last = v.scalar_tensor_tensor(out=F.ST[c + 1][:, h, :], in0=F.ST[c][:, h, :],
                                                      scalar=F.decay[:, h, c:c + 1],
                                                      in1=bank[:, c % 2, h * DV:(h + 1) * DV], op0=ALU.mult, op1=ALU.add)
                    last.then_inc(F.state_ready, 1)

                states = nch if F is A else nch - 1
                dve.sem_inc(F.state_ready, 1)
                for c in range(states):
                    state(c)
                    rows_until(AT_STATE + STATE_STEP * c)

                rows_until(AT_REC)
                for t in range(nt):
                    dve.wait_ge(F.o_out, t + 1)
                    steps(lambda: v.tensor_tensor(F.osq, F.otok[:, t, :, :], F.otok[:, t, :, :], ALU.mult))
                    steps(lambda: v.tensor_reduce(F.rms[:, t, :], F.osq, AX_X, ALU.add))
                    v.tensor_scalar(F.rms[:, t, :], F.rms[:, t, :], 1.0 / DV, RMS_EPS, ALU.mult, ALU.add).then_inc(F.ms_ready, 1)
                for t in range(nt):
                    dve.wait_ge(F.rms_root, t + 1)
                    steps(lambda: v.reciprocal(F.rms[:, t, :], F.rms[:, t, :]))
                    steps(lambda: v.tensor_tensor(F.otok[:, t, :, :], F.otok[:, t, :, :],
                                                  F.rms[:, t, :].unsqueeze(2).to_broadcast([P, HH, DV]), ALU.mult))
                    v.tensor_tensor(F.otok[:, t, :, :], F.otok[:, t, :, :],
                                    F.tok[:, t, G0:G0 + HH * DV].rearrange("p (h e) -> p h e", h=HH),
                                    ALU.mult).then_inc(F.rec_ready, 1)

                for m in range(KC):
                    rows_until(at_mix(m))
                    b = 4 * (m % 2)
                    dve.wait_ge(F.gate_ready, 2 * m + 2)
                    dve.wait_ge(F.mix_done, m + 1)
                    for k in range(2):
                        ch(v.tensor_tensor(F.sig[:, m % 2, k, :], F.sig[:, m % 2, k, :], bank[:, b + 2 + k, 0:n], ALU.mult))
                    ch.wait()
                    v.tensor_tensor(F.mixT[:, m, :], F.sig[:, m % 2, 0, :], F.sig[:, m % 2, 1, :], ALU.add).then_inc(F.mix_out, 1)

                dve.wait_ge(F.x_in, 16)
                dve.wait_ge(ln1_in, 32)
                for u, (k, t) in enumerate(out_units(F)):
                    if t == 0 and k < N_OUT - 1:
                        rows_until(AT_OUT + OUT_STEP * k)
                    dve.wait_ge(F.y_done, u + 1)
                    xs = F.x1[:, t, k * TW:(k + 1) * TW]
                    v.scalar_tensor_tensor(out=xs, in0=xs, scalar=ALPHA, in1=bank[:, u % 4, 0:TW],
                                           op0=ALU.mult, op1=ALU.add).then_inc(F.y_out, 1)
                    if k == N_OUT - 1:
                        dve.wait_ge(F.y_out, u + 1)
                        layer_norm(t, F.x1[:, t, :], F.x1[:, t, :], F.var_ready, F.std_ready, F.x1_ready)

            def layer_norm(t, src, dst, var_ready, std_ready, ready):
                for n in range(2):
                    ch(v.bn_stats(stats[:, n, :], src[:, n * 512:(n + 1) * 512]))
                ch.gate()
                steps(lambda: v.bn_aggr(mv[:, :], stats[:, :, :]))
                v.tensor_scalar(rstd[:, :], mv[:, 1:2], LN_EPS, None, ALU.add).then_inc(var_ready, 1)
                dve.wait_ge(std_ready, t + 1)
                steps(lambda: v.reciprocal(rstd[:, :], rstd[:, :]))
                steps(lambda: v.tensor_scalar(dst, src, mv[:, 0:1], rstd[:, 0:1], ALU.subtract, ALU.mult))
                steps(lambda: v.tensor_tensor(dst, dst, ln_gb[:, 0, :], ALU.mult))
                v.tensor_tensor(dst, dst, ln_gb[:, 1, :], ALU.add).then_inc(ready, 1)
                dve.wait_ge(ready, t + 1)

            eidx_all = eidx.rearrange("p t e -> p (t e)")
            s12_all = B.s12.rearrange("p t s -> p (t s)")
            x1_all = x1.rearrange("p t d -> p (t d)")

            def top16(values, best, index, n, fill):
                for half in range(2):
                    part = slice(8 * half, 8 * half + 8)
                    for b in range(n):
                        ch(v.max(best(b)[:, part], values(b)))
                    fill()
                    ch.gate()
                    for b in range(n):
                        ch(v.max_index(index(b)[:, part], best(b)[:, part], values(b)))
                    fill()
                    ch.gate()
                    if half == 0:
                        for b in range(n):
                            ch(v.match_replace(values(b), best(b)[:, part], values(b), LOWEST))
                        fill()
                        ch.gate()

            def route(hs, values, cand, onehot, store, fill=lambda: None):
                nh = len(hs)
                h0 = hs[0]
                sums = [P, nh, TOPK, TOPK]
                top16(values, lambda b: top[:, h0 + b // 2, b % 2, :], lambda b: topi[:, h0 + b // 2, b % 2, :], 2 * nh, fill)
                tp, tf = top[:, h0:h0 + nh, :, :], topf[:, h0:h0 + nh, :, :]
                steps(lambda: v.tensor_copy(tf, topi[:, h0:h0 + nh, :, :]),
                      lambda: v.tensor_tensor(cand, tp[:, :, 0, :].unsqueeze(3).to_broadcast(sums),
                                              tp[:, :, 1, :].unsqueeze(2).to_broadcast(sums), ALU.add), fill=fill)
                ch.gate()
                top16(lambda h: cand[:, h, :, :].rearrange("p i j -> p (i j)"), lambda h: sco[:, h0 + h, :],
                      lambda h: sci[:, h0 + h, :], nh, fill)
                ei = slice(h0 * TOPK, (h0 + nh) * TOPK)
                ci = sci[:, h0:h0 + nh, :].rearrange("p h k -> p (h k)")
                steps(lambda: v.tensor_scalar(half_i[:, 0, ei], ci, 4, None, ALU.logical_shift_right),
                      lambda: v.tensor_scalar(half_i[:, 1, ei], ci, 15, None, ALU.bitwise_and), fill=fill)
                steps(lambda: v.tensor_copy(half_f[:, :, ei], half_i[:, :, ei]), fill=fill)
                both = [P, 2, nh * TOPK, TOPK]
                steps(lambda: v.tensor_tensor(onehot, half_f[:, :, ei].unsqueeze(3).to_broadcast(both),
                                              iota16[:, :].unsqueeze(1).unsqueeze(1).to_broadcast(both), ALU.is_equal),
                      fill=fill)
                oh = [onehot[:, half, :, :].rearrange("p (h k) j -> p h k j", h=nh) for half in range(2)]
                steps(*[lambda half=half: v.tensor_tensor(oh[half], oh[half],
                                                          tf[:, :, half, :].unsqueeze(2).to_broadcast(sums), ALU.mult)
                        for half in range(2)], fill=fill)
                steps(lambda: v.tensor_reduce(e12[:, :, ei], onehot, AX_X, ALU.add), fill=fill)
                e1, e2 = e12[:, 0, ei], e12[:, 1, ei]
                steps(lambda: v.scalar_tensor_tensor(out=e1, in0=e1, scalar=float(NK), in1=e2, op0=ALU.mult, op1=ALU.add),
                      fill=fill)
                store(ei)

            def softmax_arg():
                v.tensor_tensor(gexp, sco, sco[:, :, 0:1].to_broadcast([P, PH, TOPK]), ALU.subtract).then_inc(gexp_arg, 1)

            def route_tile(t):
                ch.gate()
                ch(v.tensor_copy(scur.rearrange("p b k -> p (b k)"),
                                 s12_all[:, bass.ds((t - 1) * (2 * PH * NK), 2 * PH * NK)]))
                ch.gate()
                for half in range(2):
                    def store(ei):
                        ch.gate()
                        v.tensor_copy(eidx_all[:, bass.ds(t * NE + ei.start, NE // 2)], e12[:, 0, ei]).then_inc(idx_ready, PH // 2)

                    h0 = half * PH // 2
                    route(range(h0, h0 + PH // 2), lambda b: scur[:, 2 * h0 + b, :], cand, onehot, store)
                softmax_arg()

            def route_half(half):
                h0 = half * PH // 2
                dve.wait_ge(B.ks_out, (h0 + PH // 2 - 1) * B.nt + 1)
                dve.sem_inc(route_gate, 1)
                points = [0]

                def fill():
                    points[0] += 1
                    if points[0] in SHARE0_POINTS:
                        share_row(ROUNDS - 2 + half, SHARE0_POINTS.index(points[0]))

                route(range(h0, h0 + PH // 2), lambda b: B.s12[:, 0, (2 * h0 + b) * NK:(2 * h0 + b + 1) * NK], cand, onehot,
                      lambda ei: v.tensor_copy(eidx[:, 1, ei], e12[:, 0, ei]).then_inc(idx_ready, PH // 2), fill)
                assert points[0] == ROUTE_STEPS, points

            def share_row(i, g):
                s = g * GRP + GRP - 1
                j = i * SLOTS + s
                dve.wait_ge(landed[s], 16 * (ROUNDS + i + 1))
                ch.wait()
                ch(v.scalar_tensor_tensor(out=acc, in0=rows[:, s, :], scalar=wv[:, j:j + 1], in1=acc, op0=ALU.mult, op1=ALU.add))
                ch.wait()
                dve.sem_inc(v_shared, 1)

            def hidden(t):
                ch.gate()
                ch(v.tensor_copy(x1cur, x1_all[:, bass.ds(t * D, D)]))
                start = ch.n
                with dve.Fori(0, ROUNDS) as i:
                    ch.enter(i, 1)
                    for s in range(SLOTS):
                        if s == 0:
                            ch.wait()
                        dve.wait_ge(landed[s], 16 * (2 * ROUNDS * t + i + 1))
                        last = v.tensor_tensor_reduce(rows[:, s, :], rows[:, s, :], x1cur, 1.0, 0.0,
                                                      ALU.mult, ALU.add, hid_r[:, s:s + 1])
                        if s % GRP == GRP - 1:
                            last.then_inc(u_used, 1)
                    dve.wait_ge(u_used, GPP * t + GPR * i + GPR)
                    dve.sem_inc(route_gate, 1)
                    ch(v.tensor_copy(hid[:, bass.ds(i * SLOTS, SLOTS)], hid_r))
                    ch.leave(start, ROUNDS)
                ch.wait()
                dve.sem_inc(hid_ready, 1)

            def weights(t):
                dve.wait_ge(gexp_done, t + 1)
                steps(lambda: v.tensor_reduce(gsum, gexp, AX_X, ALU.add))
                steps(lambda: v.reciprocal(gsum, gsum))
                steps(lambda: v.tensor_tensor(gexp, gexp, gsum.unsqueeze(2).to_broadcast([P, PH, TOPK]), ALU.mult))
                dve.wait_ge(gelu_done, t + 1)
                v.tensor_tensor(wv, hid, gexp.rearrange("p h k -> p (h k)"), ALU.mult).then_inc(wv_ready, 1)
                dve.wait_ge(wv_ready, t + 1)

            def share(t):
                start = ch.n
                with dve.Fori(SHARE_FROM, ROUNDS) as i:
                    ch.enter(i - SHARE_FROM, GPR)
                    for s in range(GRP - 1, SLOTS, GRP):
                        dve.wait_ge(landed[s], 16 * (2 * ROUNDS * t + ROUNDS + i + 1))
                        dve.sem_inc(route_gate, 1)
                        ch.wait()
                        ch(v.scalar_tensor_tensor(out=acc, in0=rows[:, s, :], scalar=wv[:, bass.ds(i * SLOTS + s, 1)],
                                                  in1=acc, op0=ALU.mult, op1=ALU.add))
                        ch.wait()
                        dve.sem_inc(v_shared, 1)
                    ch.leave(start, ROUNDS - SHARE_FROM)

            def start_share():
                dve.sem_inc(v_shared, GPR * SHARE_FROM)
                ch(v.memset(acc, 0.0))

            def second_norm(t, count):
                dve.wait_ge(v_used, count)
                dve.wait_ge(y_free, t + 1)
                dve.sem_inc(route_gate, 1)
                steps(lambda: v.tensor_tensor(acc, acc, psum_acc, ALU.add))
                dve.sem_inc(acc_out, 1)
                layer_norm(t, acc, ybuf, var2_ready, std2_ready, y2_ready)

            psum_acc = bank[:, 0:2, :].rearrange("p b n -> p (b n)")
            forget_gates(A)
            rotate(A)
            front(A, lambda q: None)
            for h in range(PH):
                dve.wait_ge(A.ks_out, h + 1)
                dve.sem_inc(route_gate, 1)
                fills = [0]

                def fill():
                    fills[0] += 1
                    rows_until(ROUTE_ROWS * (h - 1) + ROUTE_ROWS * fills[0] // ROUTE_STEPS)

                def store(ei):
                    v.tensor_copy(eidx[:, 0, ei], e12[:, 0, ei]).then_inc(idx_ready, 1)

                route(range(h, h + 1), lambda b: A.s12[:, 0, (2 * h + b) * NK:(2 * h + b + 1) * NK],
                      cand0, onehot0, store, fill)
                assert fills[0] == ROUTE_STEPS, fills
                if h == FG_HEAD:
                    forget_gates(B)
                if h == ROPE_HEAD:
                    rotate(B)
            softmax_arg()
            dve.wait_ge(gexp_arg, 1)
            front(B, rows_until)
            rows_until(NE + EARLY_V * SLOTS)
            route_half(0)
            route_half(1)
            softmax_arg()
            dve.wait_ge(ln2_in, 32)
            start = ch.n
            with dve.Fori(1, T - 1) as t:
                ch.enter(t - 1, PER_TILE)
                hidden(t)
                weights(t)
                second_norm(t - 1, GPP * t + GPR)
                start_share()
                route_tile(t + 1)
                share(t)
                ch.leave(start, T - 2)
            hidden(T - 1)
            weights(T - 1)
            second_norm(T - 2, GPP * (T - 1) + GPR)
            start_share()
            share(T - 1)
            second_norm(T - 1, GPP * T + GPR)

        @block.gpsimd
        def _(pool):
            pool.sem_inc(v_used, GPR)
            pool.sem_inc(v_shared, GPR)
            pool.sem_inc(acc_out, 1)
            eidx_all = eidx.rearrange("p t e -> p (t e)")

            def gather(t, table, phase, i, g, free, count):
                if phase == 0 and g == 0:
                    pool.wait_ge(idx_ready, PH * t + i + 1)
                if free is v_used:
                    pool.wait_ge(v_shared, count)
                    pool.sem_inc(pool_gate, 1)
                pool.wait_ge(free, count)
                pool.sem_inc(pool_gate, 1)
                sl = slice(g * GRP, (g + 1) * GRP)
                nc.gpsimd.tensor_copy(cur[:, sl], eidx_all[:, bass.ds(t * NE + i * SLOTS + g * GRP, GRP)]).then_inc(cur_ready, 1)
                pool.wait_ge(cur_ready, 2 * GPP * t + GPP * phase + GPR * i + g + 1)
                pool.sem_inc(pool_gate, 1)
                for s in range(g * GRP, (g + 1) * GRP):
                    pool.indirect_dma_start(rows[:, s, :], None, table,
                                            bass.IndirectOffsetOnAxis(cur[:, s:s + 1], 0)).then_inc(landed[s], 16)

            with pool.Fori(0, T) as t:
                for phase, table, used, credit in ((0, u_rows, u_used, 0), (1, v_rows, v_used, GPR)):
                    for g in range(GPR):
                        if phase == 0:
                            gather(t, table, phase, 0, g, v_used, GPP * t + g + 1)
                        else:
                            gather(t, table, phase, 0, g, u_used, GPP * t + GPP - GPR + g + 1)
                    with pool.Fori(1, ROUNDS) as i:
                        for g in range(GPR):
                            gather(t, table, phase, i, g, used, credit + GPP * t + GPR * (i - 1) + g + 1)


def kernel(**inputs):
    import numpy as np
    import concourse.bacc as bacc
    from concourse.bass_utils import run_bass_kernel_spmd

    nc = bacc.Bacc("TRN2", target_bir_lowering=False, num_devices=1)
    arrays = {}

    def dram(name, a):
        a = np.ascontiguousarray(a)
        arrays[name] = a
        return nc.dram_tensor(name, a.shape, mybir.dt.from_np(a.dtype), kind="ExternalInput").ap()

    def get(name):
        return np.asarray(inputs[name])

    def blocks(w, n):
        return w.reshape(w.shape[0] // P, P, n, w.shape[1] // n).transpose(2, 1, 0, 3).reshape(n, P, -1)

    x = get("x")[0]
    w_in = get("w_in")[0]
    widths = (HEADS * HD, KVH * HD, KVH * HD, HH * DK, HH * DK, HH * DV, HH * DV, D, D)
    q, k, v, hq, hf, hi, hg, ga, gh = np.split(w_in, np.cumsum(widths)[:-1], axis=1)
    gates = [blocks(w, KC) for w in (ga, gh)]
    branch = [blocks(get(n)[0], KC) for n in ("w_proj_attn", "w_proj_hgrn")]
    mix = []
    for m in range(0, KC, 2):
        mix += [np.concatenate([g[k] for g in gates], axis=1) for k in (m, m + 1)]
        mix.append(np.concatenate([w[k] for k in (m, m + 1) for w in branch], axis=1))
    items = np.concatenate([blocks(np.concatenate([hf, hq], axis=1), N_HQF),
                            blocks(np.concatenate([q, k, v, hi, hg], axis=1), N_TOK), np.stack(mix),
                            blocks(get("w_out")[0], N_OUT), blocks(get("peer_wq")[0], N_WQ)])
    causal = np.kron(np.eye(2, dtype=np.uint32), np.triu(np.ones((CH, CH), np.uint32)))
    chunk = np.tile((np.arange((T - 1) * P) % CH != 0).astype(np.float32), (P, 1))
    freq = (np.float32(500000.0) ** (-np.arange(0, ROT, 2, dtype=np.float32) / np.float32(ROT))).astype(np.float32)
    args = [
        dram("x_d", x), dram("xT_d", x.T),
        dram("w_items_d", items),
        dram("keysT_d", get("peer_keys")[0].transpose(2, 0, 1)),
        dram("pos_d", get("positions")[0].reshape(T, P).T),
        dram("freq_d", freq),
        dram("sinks_d", get("attn_sinks")[0].reshape(PAIRS, 2).T),
        dram("lb_d", get("hgrn_lb").reshape(2, HH, DK).transpose(2, 0, 1)),
        dram("norm_g_d", get("hgrn_norm_g")[0]),
        dram("ln1_d", np.stack([get("ln1_g")[0], get("ln1_b")[0]])),
        dram("ln2_d", np.stack([get("ln2_g")[0], get("ln2_b")[0]])),
        dram("ident_d", np.eye(P, dtype=np.float32)), dram("causal_d", causal), dram("chunk_d", chunk),
        dram("iota_d", np.tile(np.arange(TOPK, dtype=np.float32), (P, 1))),
        dram("u_d", get("peer_u")[0]), dram("v_d", get("peer_v")[0]),
    ]
    out = nc.dram_tensor("out_d", (S, D), F32, kind="ExternalOutput").ap()
    build(nc, *args, out)
    r = run_bass_kernel_spmd(nc, [arrays], core_ids=[0])
    return r.results[0]["out_d"].reshape(1, S, D)
```
